# Optimizing a Trainium2 kernel written in Bass

```python
import jax
import jax.numpy as jnp
from jax import lax
import numpy as np

D_MODEL = 1024
BATCH = 1
SEQ = 128
DEPTH = 2
DEC_BATCH = 1
DEC_SEQ = 512
PAST_LEN = 256

GRID_W = 64
HEAD_DIM = 64
A_HEADS = 8
A_KV_HEADS = 2
B_HEADS = 8
C_HEADS = 16
A_WIDTH = A_HEADS * HEAD_DIM
A_KV_WIDTH = A_KV_HEADS * HEAD_DIM
B_WIDTH = B_HEADS * HEAD_DIM
C_WIDTH = C_HEADS * HEAD_DIM
DECAY_LORA = 64
ICLR_LORA = 64
GATE_LORA = 128
B_SHIFT_WIDTH = 3 * B_WIDTH + 2 * DECAY_LORA + 2 * ICLR_LORA + GATE_LORA
EVEN_IN = A_WIDTH + 2 * A_KV_WIDTH + B_SHIFT_WIDTH
EVEN_SPLITS = (A_WIDTH, A_WIDTH + A_KV_WIDTH, A_WIDTH + 2 * A_KV_WIDTH)
B_SPLITS = (B_WIDTH, 2 * B_WIDTH, 3 * B_WIDTH, 3 * B_WIDTH + DECAY_LORA, 3 * B_WIDTH + 2 * DECAY_LORA,
            3 * B_WIDTH + 2 * DECAY_LORA + ICLR_LORA, 3 * B_WIDTH + 2 * DECAY_LORA + 2 * ICLR_LORA)
NA_ROWS = 8
NA_COLS = 16
D_FF = 2816
N_EXPERTS = 8
TOP_K = 2
D_EXPERT = 1408
N_EVEN = (DEPTH + 1) // 2
N_ODD = DEPTH // 2
Q_BLOCK = 128
ROPE_THETA = 10000.0
EPS = 1e-6
GN_EPS = 64e-5
NEG_INF = -1e30

kernel_name = 'hybrid_diffusion_prefix_trunk_step'

def rmsnorm(x, g):
    x32 = x.astype(jnp.float32)
    y = x32 * lax.rsqrt(jnp.mean(x32 * x32, axis=-1, keepdims=True) + EPS)
    return (y * g.astype(jnp.float32)).astype(x.dtype)

def adaln(cond, w, b):
    return jnp.split(jax.nn.silu(cond) @ w + b, 6, axis=-1)

def modulate(x, g, shift, scale):
    return rmsnorm(x, g) * (1 + scale[:, None]) + shift[:, None]

def token_shift_mix(z, mu):
    zp = jnp.pad(z, ((0, 0), (1, 1), (0, 0)))
    return z + mu * (0.5 * (zp[:, :-2] + zp[:, 2:]) - z)

def axial_rope(x):
    T, dh = x.shape[1], x.shape[-1]
    t = np.arange(T)
    n_f = dh // 4
    inv = ROPE_THETA ** (-np.arange(n_f, dtype=np.float32) / n_f)

    def rot(xa, pos):
        ang = pos[:, None].astype(np.float32) * inv[None, :]
        cos = jnp.asarray(np.cos(ang), x.dtype)[None, :, None, :]
        sin = jnp.asarray(np.sin(ang), x.dtype)[None, :, None, :]
        x1, x2 = xa[..., :n_f], xa[..., n_f:]
        return jnp.concatenate([x1 * cos - x2 * sin, x1 * sin + x2 * cos], axis=-1)

    half = dh // 2
    return jnp.concatenate([rot(x[..., :half], t // GRID_W), rot(x[..., half:], t % GRID_W)], axis=-1)

def gqa_attention(q, k, v):
    B, T, Hq, dh = q.shape
    Hkv = k.shape[2]
    G = Hq // Hkv
    nb = T // Q_BLOCK
    qb = q.reshape(B, nb, Q_BLOCK, Hkv, G, dh).transpose(1, 0, 2, 3, 4, 5)
    scale = dh ** -0.5

    def block(qi):
        s = jnp.einsum('bqkgd,bskd->bkgqs', qi, k).astype(jnp.float32) * scale
        p = jax.nn.softmax(s, axis=-1).astype(v.dtype)
        return jnp.einsum('bkgqs,bskd->bqkgd', p, v)

    o = lax.map(block, qb)
    return o.transpose(1, 0, 2, 3, 4, 5).reshape(B, T, Hq, dh)

def neighbourhood_attention(q, k, v, ck, cv, rpb):
    B, T, H, dh = q.shape
    rows = T // GRID_W
    kh = min(NA_ROWS, rows)
    kw = NA_COLS
    r = np.arange(rows)
    row_idx = np.clip(r - kh // 2, 0, rows - kh)[:, None] + np.arange(kh)[None, :]
    col = np.arange(GRID_W)
    cs = np.clip(col - kw // 2, 0, GRID_W - kw)
    col_in = (col[None, :] >= cs[:, None]) & (col[None, :] < cs[:, None] + kw)
    dr = row_idx - r[:, None] + (NA_ROWS - 1)
    dc = np.clip(col[None, :] - col[:, None], -(NA_COLS - 1), NA_COLS - 1) + (NA_COLS - 1)
    scale = dh ** -0.5
    qg = q.reshape(B, rows, GRID_W, H, dh)
    kg = k.reshape(B, rows, GRID_W, H, dh)[:, row_idx]
    vg = v.reshape(B, rows, GRID_W, H, dh)[:, row_idx]
    bias = rpb[:, dr[:, None, :, None], dc[None, :, None, :]].astype(jnp.float32)
    s_nb = jnp.einsum('brqhd,brkwhd->bhrqkw', qg, kg).astype(jnp.float32) * scale + bias[None]
    s_nb = jnp.where(jnp.asarray(col_in)[:, None, :], s_nb, NEG_INF)
    s_nb = s_nb.reshape(B, H, rows, GRID_W, kh * GRID_W)
    s_ctx = jnp.einsum('brqhd,bshd->bhrqs', qg, ck).astype(jnp.float32) * scale
    p = jax.nn.softmax(jnp.concatenate([s_nb, s_ctx], axis=-1), axis=-1).astype(v.dtype)
    p_nb = p[..., :kh * GRID_W].reshape(B, H, rows, GRID_W, kh, GRID_W)
    p_ctx = p[..., kh * GRID_W:]
    o = jnp.einsum('bhrqkw,brkwhd->brqhd', p_nb, vg) + jnp.einsum('bhrqs,bshd->brqhd', p_ctx, cv)
    return o.reshape(B, T, H, dh)

def _rwkv_step(S, xs):
    r, w, k, v, kk, a = xs
    sa = jnp.einsum('bhij,bhj->bhi', S, -kk)
    S = S * w[:, :, None, :] + sa[..., None] * (kk * a)[:, :, None, :] + v[..., None] * k[:, :, None, :]
    return S, jnp.einsum('bhij,bhj->bhi', S, r)

def rwkv7_bidir(zb, s0f, s0b, W, e):
    B, T, _ = zb.shape
    f32 = jnp.float32
    r, k, v, wdf, wdb, adf, adb, gd = jnp.split(zb, B_SPLITS, axis=-1)
    kk = (k * W['b_kk'][e]).reshape(B, T, B_HEADS, HEAD_DIM).astype(f32)
    kk = kk * lax.rsqrt(jnp.sum(kk * kk, axis=-1, keepdims=True) + 1e-12)
    kk_t = kk.transpose(1, 0, 2, 3)

    def heads_t(t):
        return t.reshape(B, T, B_HEADS, HEAD_DIM).astype(f32).transpose(1, 0, 2, 3)

    r_t, v_t = heads_t(r), heads_t(v)

    def direction(wd, ad, d, s0, reverse):
        wl = (W['b_w0'][e, d] + jnp.tanh(wd) @ W['b_w2'][e, d]).astype(f32)
        decay = jnp.exp(-jnp.exp(-jax.nn.softplus(-wl) - 0.5))
        a = jax.nn.sigmoid(W['b_a0'][e, d] + ad @ W['b_a2'][e, d])
        kd = k * (1 + (a - 1) * W['b_ka'][e])
        xs = (r_t, heads_t(decay), heads_t(kd), v_t, kk_t, heads_t(a))
        s, ys = lax.scan(_rwkv_step, s0.astype(f32), xs, reverse=reverse)
        return ys, s

    yf, sf = direction(wdf, adf, 0, s0f, False)
    yb, sb = direction(wdb, adb, 1, s0b, True)
    y = (yf + yb).transpose(1, 0, 2, 3)
    mu = jnp.mean(y, axis=-1, keepdims=True)
    var = jnp.mean(jnp.square(y - mu), axis=-1, keepdims=True)
    y = ((y - mu) * lax.rsqrt(var + GN_EPS)).reshape(B, T, B_WIDTH)
    y = (y * W['b_ln_g'][e] + W['b_ln_b'][e]).astype(zb.dtype)
    rh = r.reshape(B, T, B_HEADS, HEAD_DIM)
    kh_ = k.reshape(B, T, B_HEADS, HEAD_DIM)
    vh = v.reshape(B, T, B_HEADS, HEAD_DIM)
    bonus = (jnp.sum(rh * kh_ * W['b_rk'][e], axis=-1, keepdims=True) * vh).reshape(B, T, B_WIDTH)
    g = jax.nn.sigmoid(gd) @ W['b_g2'][e]
    return (y + bonus) * g, sf.astype(zb.dtype), sb.astype(zb.dtype)

def even_mixer(h, e, W, ctx):
    B, T, _ = h.shape
    z = h @ W['w_in_e'][e]
    qa, ka, va, zb = jnp.split(z, EVEN_SPLITS, axis=-1)
    q = rmsnorm(qa.reshape(B, T, A_HEADS, HEAD_DIM), W['a_q_gain'][e])
    k = rmsnorm(ka.reshape(B, T, A_KV_HEADS, HEAD_DIM), W['a_k_gain'][e])
    v = va.reshape(B, T, A_KV_HEADS, HEAD_DIM)
    if ctx is None:
        ya = gqa_attention(q, k, v)
        s0f = jnp.zeros((B, B_HEADS, HEAD_DIM, HEAD_DIM), jnp.float32)
        s0b = s0f
    else:
        ck, cv, s0f, s0b = ctx
        ya = gqa_attention(axial_rope(q), jnp.concatenate([axial_rope(k), ck], axis=1),
                           jnp.concatenate([v, cv], axis=1))
    yb, sf, sb = rwkv7_bidir(token_shift_mix(zb, W['b_mu'][e]), s0f, s0b, W, e)
    out = jnp.concatenate([ya.reshape(B, T, A_WIDTH), yb], axis=-1) @ W['w_out_e'][e]
    return out, (k, v, sf, sb)

def odd_mixer(h, o, W, ctx):
    B, T, _ = h.shape
    q, k, v = [t.reshape(B, T, C_HEADS, HEAD_DIM) for t in jnp.split(h @ W['w_in_o'][o], 3, axis=-1)]
    if ctx is None:
        y = gqa_attention(q, k, v)
    else:
        ck, cv = ctx
        y = neighbourhood_attention(q, k, v, ck, cv, W['c_rpb'][o])
    return y.reshape(B, T, C_WIDTH) @ W['w_out_o'][o], (k, v)

def swiglu(x, w_gu, w_dn):
    g, u = jnp.split(x @ w_gu, 2, axis=-1)
    return (jax.nn.silu(g) * u) @ w_dn

def moe_swiglu(h, router_w, router_b, w_gu, w_dn):
    B, T, D = h.shape
    xf = h.reshape(B * T, D)
    logits = (xf @ router_w).astype(jnp.float32)
    _, idx = lax.top_k(logits + router_b.astype(jnp.float32), TOP_K)
    wts = jax.nn.softmax(jnp.take_along_axis(logits, idx, axis=-1), axis=-1)
    gates = jnp.sum(jax.nn.one_hot(idx, N_EXPERTS, dtype=jnp.float32) * wts[..., None], axis=1).astype(h.dtype)
    y = jnp.zeros_like(xf)
    for ex in range(N_EXPERTS):
        y = y + gates[:, ex:ex + 1] * swiglu(xf, w_gu[ex], w_dn[ex])
    return y.reshape(B, T, D)

def trunk_layer(l, x, cond, W, ctx):
    sh1, sc1, g1, sh2, sc2, g2 = adaln(cond, W['ada_w'][l], W['ada_b'][l])
    h = modulate(x, W['norm1_g'][l], sh1, sc1)
    if l % 2 == 0:
        out, new = even_mixer(h, l // 2, W, ctx)
    else:
        out, new = odd_mixer(h, l // 2, W, ctx)
    x = x + g1[:, None] * out
    h = modulate(x, W['norm2_g'][l], sh2, sc2)
    if l % 2 == 0:
        f = swiglu(h, W['ffn_w_gu'][l // 2], W['ffn_w_dn'][l // 2])
    else:
        o = l // 2
        f = moe_swiglu(h, W['router_w'][o], W['router_b'][o], W['moe_w_gu'][o], W['moe_w_dn'][o])
    x = x + g2[:, None] * f
    return x, new

def setup_inputs(seed: int = 0) -> dict:
    key = jax.random.key(seed)
    ks = iter(jax.random.split(key, 48))

    def nrm(shape, scale):
        return jax.random.normal(next(ks), shape, jnp.float32) * scale

    D = D_MODEL
    return {
        'x_prompt': nrm((BATCH, SEQ, D), 1.0),
        'x_sample': nrm((DEC_BATCH, DEC_SEQ, D), 1.0),
        'cache_a_k': nrm((DEC_BATCH, N_EVEN, PAST_LEN, A_KV_HEADS, HEAD_DIM), 1.0),
        'cache_a_v': nrm((DEC_BATCH, N_EVEN, PAST_LEN, A_KV_HEADS, HEAD_DIM), 1.0),
        'state_b_fwd': nrm((DEC_BATCH, N_EVEN, B_HEADS, HEAD_DIM, HEAD_DIM), 0.3),
        'state_b_bwd': nrm((DEC_BATCH, N_EVEN, B_HEADS, HEAD_DIM, HEAD_DIM), 0.3),
        'cache_c_k': nrm((DEC_BATCH, N_ODD, PAST_LEN, C_HEADS, HEAD_DIM), 1.0),
        'cache_c_v': nrm((DEC_BATCH, N_ODD, PAST_LEN, C_HEADS, HEAD_DIM), 1.0),
        'c': nrm((DEC_BATCH, D), 1.0),
        'c_ctx': nrm((D,), 1.0),
        'ada_w': nrm((DEPTH, D, 6 * D), D ** -0.5),
        'ada_b': nrm((DEPTH, 6 * D), 0.02),
        'norm1_g': 1.0 + nrm((DEPTH, D), 0.02),
        'norm2_g': 1.0 + nrm((DEPTH, D), 0.02),
        'final_norm_g': 1.0 + nrm((D,), 0.02),
        'w_in_e': nrm((N_EVEN, D, EVEN_IN), D ** -0.5),
        'w_out_e': nrm((N_EVEN, A_WIDTH + B_WIDTH, D), (A_WIDTH + B_WIDTH) ** -0.5),
        'a_q_gain': 1.0 + nrm((N_EVEN, HEAD_DIM), 0.02),
        'a_k_gain': 1.0 + nrm((N_EVEN, HEAD_DIM), 0.02),
        'b_mu': jax.random.uniform(next(ks), (N_EVEN, B_SHIFT_WIDTH), jnp.float32),
        'b_w0': nrm((N_EVEN, 2, B_WIDTH), 0.5) - 0.5,
        'b_w2': nrm((N_EVEN, 2, DECAY_LORA, B_WIDTH), 0.5 * DECAY_LORA ** -0.5),
        'b_a0': nrm((N_EVEN, 2, B_WIDTH), 0.1),
        'b_a2': nrm((N_EVEN, 2, ICLR_LORA, B_WIDTH), 0.5 * ICLR_LORA ** -0.5),
        'b_g2': nrm((N_EVEN, GATE_LORA, B_WIDTH), GATE_LORA ** -0.5),
        'b_kk': 0.85 + nrm((N_EVEN, B_WIDTH), 0.05),
        'b_ka': 1.0 + nrm((N_EVEN, B_WIDTH), 0.05),
        'b_rk': nrm((N_EVEN, B_HEADS, HEAD_DIM), 0.05),
        'b_ln_g': 1.0 + nrm((N_EVEN, B_WIDTH), 0.02),
        'b_ln_b': nrm((N_EVEN, B_WIDTH), 0.02),
        'ffn_w_gu': nrm((N_EVEN, D, 2 * D_FF), D ** -0.5),
        'ffn_w_dn': nrm((N_EVEN, D_FF, D), D_FF ** -0.5),
        'w_in_o': nrm((N_ODD, D, 3 * C_WIDTH), D ** -0.5),
        'w_out_o': nrm((N_ODD, C_WIDTH, D), C_WIDTH ** -0.5),
        'c_rpb': nrm((N_ODD, C_HEADS, 2 * NA_ROWS - 1, 2 * NA_COLS - 1), 0.1),
        'router_w': nrm((N_ODD, D, N_EXPERTS), D ** -0.5),
        'router_b': nrm((N_ODD, N_EXPERTS), 0.01),
        'moe_w_gu': nrm((N_ODD, N_EXPERTS, D, 2 * D_EXPERT), D ** -0.5),
        'moe_w_dn': nrm((N_ODD, N_EXPERTS, D_EXPERT, D), D_EXPERT ** -0.5),
    }

def reference(x_prompt, x_sample, cache_a_k, cache_a_v, state_b_fwd, state_b_bwd, cache_c_k, cache_c_v,
              c, c_ctx, ada_w, ada_b, norm1_g, norm2_g, final_norm_g, w_in_e, w_out_e, a_q_gain, a_k_gain,
              b_mu, b_w0, b_w2, b_a0, b_a2, b_g2, b_kk, b_ka, b_rk, b_ln_g, b_ln_b, ffn_w_gu, ffn_w_dn,
              w_in_o, w_out_o, c_rpb, router_w, router_b, moe_w_gu, moe_w_dn):
    W = {'ada_w': ada_w, 'ada_b': ada_b, 'norm1_g': norm1_g, 'norm2_g': norm2_g,
         'w_in_e': w_in_e, 'w_out_e': w_out_e, 'a_q_gain': a_q_gain, 'a_k_gain': a_k_gain,
         'b_mu': b_mu, 'b_w0': b_w0, 'b_w2': b_w2, 'b_a0': b_a0, 'b_a2': b_a2, 'b_g2': b_g2,
         'b_kk': b_kk, 'b_ka': b_ka, 'b_rk': b_rk, 'b_ln_g': b_ln_g, 'b_ln_b': b_ln_b,
         'ffn_w_gu': ffn_w_gu, 'ffn_w_dn': ffn_w_dn, 'w_in_o': w_in_o, 'w_out_o': w_out_o,
         'c_rpb': c_rpb, 'router_w': router_w, 'router_b': router_b,
         'moe_w_gu': moe_w_gu, 'moe_w_dn': moe_w_dn}

    x_ctx = x_prompt
    a_k, a_v, s_f, s_b, c_k, c_v = [], [], [], [], [], []
    for l in range(DEPTH):
        x_ctx, new = trunk_layer(l, x_ctx, c_ctx[None, :], W, None)
        if l % 2 == 0:
            a_k.append(new[0]); a_v.append(new[1]); s_f.append(new[2]); s_b.append(new[3])
        else:
            c_k.append(new[0]); c_v.append(new[1])
    y_prompt = rmsnorm(x_ctx, final_norm_g)
    new_cache_a_k = jnp.stack(a_k, axis=1)
    new_cache_a_v = jnp.stack(a_v, axis=1)
    new_state_b_fwd = jnp.stack(s_f, axis=1)
    new_state_b_bwd = jnp.stack(s_b, axis=1)
    new_cache_c_k = jnp.stack(c_k, axis=1)
    new_cache_c_v = jnp.stack(c_v, axis=1)

    x_lat = x_sample
    for l in range(DEPTH):
        if l % 2 == 0:
            e = l // 2
            ctx = (cache_a_k[:, e], cache_a_v[:, e], state_b_fwd[:, e], state_b_bwd[:, e])
        else:
            o = l // 2
            ctx = (cache_c_k[:, o], cache_c_v[:, o])
        x_lat, _ = trunk_layer(l, x_lat, c, W, ctx)
    y_sample = rmsnorm(x_lat, final_norm_g)

    return (y_prompt, y_sample, new_cache_a_k, new_cache_a_v, new_state_b_fwd, new_state_b_bwd,
            new_cache_c_k, new_cache_c_v)


_drawn_inputs = setup_inputs


def setup_inputs(seed=0):
    import zlib

    import numpy as np

    out = dict(_drawn_inputs(seed))
    spreads = {}
    factors = {'state_b_fwd': 21.571,
     'state_b_bwd': 17.731,
     'final_norm_g': 22.517,
     'a_q_gain': 5.002,
     'a_k_gain': 2.861,
     'b_ln_g': 2.958,
     'b_ln_b': 8.753,
     'c_rpb': 17.997,
     'cache_a_k': 8.0,
     'cache_a_v': 8.0,
     'router_b': 2.902,
     'cache_c_k': 3.007,
     'cache_c_v': 2.998}
    for name, (base, spread) in spreads.items():
        noise = np.random.default_rng([zlib.crc32(name.encode()), seed]).standard_normal(out[name].shape)
        drawn = base * np.exp(spread * noise) if base else spread * noise
        out[name] = jnp.asarray(drawn.astype(out[name].dtype))
    for name, factor in factors.items():
        out[name] = (out[name] * factor).astype(out[name].dtype)
    return out
```

```python
from contextlib import ExitStack

import numpy as np
import concourse.bass as bass
from concourse import mybir

ALU = mybir.AluOpType
ACT = mybir.ActivationFunctionType
AX = mybir.AxisListType
F32 = mybir.dt.float32
F32R = mybir.dt.float32r
I32 = mybir.dt.int32
U32 = mybir.dt.uint32

P = 128
D = 1024
NT = 5
T = NT * P
J = D // P
HD = 64
A_HEADS, A_KV = 8, 2
C_HEADS = 16
B_HEADS = 8
CACHE = 256
EVEN_IN = 2688
QKV_E = 768
ZB = EVEN_IN - QKV_E
ZT = ZB // P
D_FF = 2816
D_EXPERT = 1408
N_EXP = 8
EPS = 1e-6
GN_EPS = 64e-5
SCALE = HD ** -0.5
DECAY = float(np.exp(-0.5))
SLOT_TILES = 17
SLOTS = (SLOT_TILES + 2) * P

RAW = 4
SPLIT = 2
UNIT = 2 * 512
MRAW, MSPLIT = 9, 3
MUNIT = 2 * 2 * 352
ECH = 352


class Signal:

    def __init__(self, nc, ctx, name):
        self.sem = ctx.enter_context(nc.semaphore(name))
        self.base = 0

    def at(self, n):
        return self.base + n


class Kit:

    def __init__(self, nc, ctx, I, O):
        self.nc, self.ctx, self.I, self.O = nc, ctx, I, O
        self.signals, self.buffers = {}, 0

    def sig(self, name):
        if name not in self.signals:
            self.signals[name] = Signal(self.nc, self.ctx, name)
        return self.signals[name]

    def unique(self, name):
        self.buffers += 1
        return f"{name}_{self.buffers}"

    def sb(self, ctx, name, shape, dt=F32):
        return ctx.enter_context(self.nc.sbuf_tensor(self.unique(name), shape, dt))

    def ps(self, ctx, name, shape, dt=F32):
        return ctx.enter_context(self.nc.psum_tensor(self.unique(name), shape, dt))

    def transposed_rows(self, ctx):
        self.h_hi = self.sb(ctx, "h_hi", [P, J, T], F32R)
        self.h_lo = self.sb(ctx, "h_lo", [P, J, T], F32R)

    def dram(self, name, shape, dt=F32):
        return self.nc.dram_tensor("scratch_" + name, shape, dt).ap()


def rows_by_partition(w):
    return w.rearrange("(p j) n -> p j n", j=J)


def rows_by_block(w):
    return w.rearrange("(j p) n -> p j n", p=P)



class Gemm:

    def __init__(self, K, ctx, chunks, units, width, sources, hi, lo, parts=1):
        self.parts = parts
        self.K, self.chunks, self.units, self.width = K, chunks, units, width
        self.sources, self.hi_in, self.lo_in = sources, hi, lo
        self.raw = K.sb(ctx, "w_raw", [P, RAW, UNIT])
        self.w_hi = K.sb(ctx, "w_hi", [P, SPLIT, UNIT], F32R)
        self.w_lo = K.sb(ctx, "w_lo", [P, SPLIT, UNIT], F32R)
        self.acc = K.ps(ctx, "acc", [P, NT, 512])
        self.landed = [K.sig(f"gemm_landed{s}") for s in range(RAW)]
        self.hi, self.lo, self.used = K.sig("gemm_hi"), K.sig("gemm_lo"), K.sig("gemm_used")
        self.sum, self.drained = K.sig("gemm_sum"), K.sig("gemm_drained")

    def view(self, ring, slot):
        return ring[:, slot, 0:2 * self.width].rearrange("p (j n) -> p j n", j=2)

    def slot_use(self, c, k, ring):
        if isinstance(c, int):
            u = c * self.units + k
            return u % ring, u // ring
        assert self.units % ring == 0
        return k % ring, c * (self.units // ring) + k // ring

    def load(self, eng, c, k):
        slot, use = self.slot_use(c, k, RAW)
        eng.wait_ge(self.lo.sem, self.lo.at(c * self.units + (k - RAW + 1)))
        for cols, src in self.sources(c, k):
            eng.dma_start(self.view(self.raw, slot)[:, :, cols], src).then_inc(self.landed[slot].sem, 16)

    def split_hi(self, eng, c, k):
        slot, use = self.slot_use(c, k, RAW)
        part, _ = self.slot_use(c, k, SPLIT)
        n = 16 * self.parts
        eng.wait_ge(self.landed[slot].sem, self.landed[slot].at(use * n + n))
        eng.wait_ge(self.used.sem, self.used.at(c * self.units + (k - SPLIT + 1)))
        eng.activation(self.w_hi[:, part, 0:2 * self.width], self.raw[:, slot, 0:2 * self.width],
                       ACT.Copy).then_inc(self.hi.sem, 1)

    def split_lo(self, eng, c, k):
        slot, _ = self.slot_use(c, k, RAW)
        part, _ = self.slot_use(c, k, SPLIT)
        eng.wait_ge(self.hi.sem, self.hi.at(c * self.units + (k + 1)))
        eng.tensor_tensor(self.w_lo[:, part, 0:2 * self.width], self.raw[:, slot, 0:2 * self.width],
                          self.w_hi[:, part, 0:2 * self.width], ALU.subtract).then_inc(self.lo.sem, 1)

    def products(self, eng, c, k):
        part, _ = self.slot_use(c, k, SPLIT)
        whi, wlo = self.view(self.w_hi, part), self.view(self.w_lo, part)
        eng.wait_ge(self.lo.sem, self.lo.at(c * self.units + (k + 1)))
        for b in range(2):
            first, last = k == 0 and b == 0, k == self.units - 1 and b == 1
            for t in range(NT):
                if first:
                    eng.wait_ge(self.drained.sem, self.drained.at(c * NT + (t - NT + 1)))
                out = self.acc[:, t, 0:self.width]
                hi, lo = self.hi_in(2 * k + b, t), self.lo_in(2 * k + b, t)
                eng.matmul(out, hi, whi[:, b, :], start=first, stop=False)
                eng.matmul(out, hi, wlo[:, b, :], start=False, stop=False)
                mm = eng.matmul(out, lo, whi[:, b, :], start=False, stop=last)
                if last and t < NT - 1:
                    mm.then_inc(self.sum.sem, 1)
        mm.then_inc(self.used.sem, 1)

    def wait_sum(self, eng, c, t):
        if t < NT - 1:
            eng.wait_ge(self.sum.sem, self.sum.at(c * (NT - 1) + (t + 1)))
        else:
            eng.wait_ge(self.used.sem, self.used.at(c * self.units + self.units))

    def end(self):
        units = self.chunks * self.units
        for s, sig in enumerate(self.landed):
            sig.base += 16 * self.parts * ((units - s + RAW - 1) // RAW)
        self.hi.base += units
        self.lo.base += units
        self.used.base += units
        self.sum.base += self.chunks * (NT - 1)
        self.drained.base += self.chunks * NT

    def each_unit(self, eng, step, behind={}):
        def chunk(c, first=False):
            for k in range(self.units):
                step(eng, c, k)
                if k in behind and not first:
                    behind[k](c - 1)
        chunk(0, first=True)
        if self.units % RAW == 0 and self.chunks > 2:
            with eng.Fori(1, self.chunks) as c:
                chunk(c)
        else:
            for c in range(1, self.chunks):
                chunk(c)
        for k in sorted(behind):
            behind[k](self.chunks - 1)



def prime(K):
    with K.nc.Block() as block:
        @block.tensor
        def _(pe):
            pe.sem_inc(K.sig("gemm_lo").sem, RAW)
            pe.sem_inc(K.sig("gemm_used").sem, SPLIT)
            pe.sem_inc(K.sig("gemm_drained").sem, NT)
            pe.sem_inc(K.sig("m_lo").sem, MRAW)
            pe.sem_inc(K.sig("m_used").sem, MSPLIT)
            pe.sem_inc(K.sig("m_act").sem, 2)
            pe.sem_inc(K.sig("m_y").sem, 1)
            pe.sem_inc(K.sig("m_stored").sem, 16)

        @block.vector
        def _(dve):
            dve.memset(K.ones[:], 1.0)

        @block.gpsimd
        def _(pool):
            pool.memset(K.minus_half[:], -0.5)
    K.sig("gemm_lo").base += RAW
    K.sig("gemm_used").base += SPLIT
    K.sig("gemm_drained").base += NT
    K.sig("m_lo").base += MRAW
    K.sig("m_used").base += MSPLIT
    K.sig("m_act").base += 2
    K.sig("m_y").base += 1
    K.sig("m_stored").base += 16



def adaln_stage(K):
    nc, I = K.nc, K.I
    RING, PARTS, CH, N = 3, 4, 512, 2 * 6 * D // 512
    HJ = J // 2
    with ExitStack() as ctx:
        cond = K.sb(ctx, "cond", [P, 2, J])
        act = K.sb(ctx, "cond_silu", [P, J, 2])
        a_hi, a_lo = (K.sb(ctx, "cond_" + n, [P, J, P], F32R) for n in ("hi", "lo"))
        bias = K.sb(ctx, "ada_bias", [2, 12 * D])
        w = K.sb(ctx, "ada_w", [P, RING, J * CH])
        w_hi, w_lo = (K.sb(ctx, "ada_w_" + n, [P, PARTS, HJ * CH], F32R) for n in ("hi", "lo"))
        row = K.sb(ctx, "mod_row", [2, 2, CH])
        acc = K.ps(ctx, "ada", [P, 2, 512])
        loaded, also, moved, cond_ready, cleared = K.sig("loaded"), K.sig("also_loaded"), K.sig("x_moved"), K.sig("cond_ready"), K.sig("shift_cleared")
        landed = [K.sig(f"ada_landed{s}") for s in range(RING)]
        split_hi, split_lo = K.sig("norm_hi"), K.sig("norm_lo")
        summed, drained = K.sig("ada_sum"), K.sig("ada_drained")
        stored = [K.sig(f"ada_stored{s}") for s in range(2)]
        ada_w = [rows_by_partition(I["ada_w"][l]) for l in range(2)]
        per_layer = N // 2

        def columns(ring, u, j):
            return ring[:, u % PARTS, j * CH:(j + 1) * CH]

        def half(u):
            return w[:, (u // 2) % RING, (u % 2) * HJ * CH:(u % 2 + 1) * HJ * CH]

        with nc.Block() as block:
            @block.sync
            def _(sp):
                sp.dma_start(cond[:, 0, :], I["c_ctx"].rearrange("(p j) -> p j", j=J)).then_inc(loaded.sem, 16)
                sp.dma_start(cond[:, 1, :], I["c"][0].rearrange("(p j) -> p j", j=J)).then_inc(loaded.sem, 16)
                for n in range(N):
                    if n >= RING:
                        sp.wait_ge(split_lo.sem, split_lo.at(2 * (n - RING + 1)))
                    l, k = divmod(n, per_layer)
                    dst = w[:, n % RING].rearrange("p (j n) -> p j n", j=J)
                    sp.dma_start(dst, ada_w[l][:, :, k * CH:(k + 1) * CH]).then_inc(landed[n % RING].sem, 16)
                    if n == 1:
                        for b in range(2):
                            sp.dma_start(bias[b:b + 1, :], I["ada_b"].rearrange("(o l) n -> o (l n)", o=1)).then_inc(also.sem, 16)
                sp.dma_start(K.ident[:], I["const_ident"]).then_inc(moved.sem, 16)
                sp.dma_start(K.x[:, 0, :], I["x_prompt"][0]).then_inc(moved.sem, 16)
                for t in range(1, NT):
                    sp.dma_start(K.x[:, t, :], I["x_sample"][0, (t - 1) * P:t * P, :]).then_inc(moved.sem, 16)
                sp.wait_ge(moved.sem, moved.at(16 * (NT + 1)))

            @block.gpsimd
            def _(pool):
                pool.memset(a_hi[:].bitcast(F32), 0.0).then_inc(cleared.sem, 1)
                pool.memset(a_lo[:].bitcast(F32), 0.0).then_inc(cleared.sem, 1)

            @block.scalar
            def _(a):
                def store(n):
                    a.wait_ge(drained.sem, drained.at(n + 1))
                    a.dma_start(K.mods[:, n * CH:(n + 1) * CH], row[:, n % 2, :]).then_inc(stored[n % 2].sem, 16)

                a.wait_ge(loaded.sem, loaded.at(32))
                a.activation(act[:].rearrange("p j c -> p c j"), cond[:], ACT.Silu).then_inc(cond_ready.sem, 1)
                a.wait_ge(cond_ready.sem, cond_ready.at(1))
                a.wait_ge(cleared.sem, cleared.at(2))
                a.activation(a_hi[:, :, 0:2], act[:], ACT.Copy).then_inc(cond_ready.sem, 1)
                for n in range(N):
                    a.wait_ge(landed[n % RING].sem, landed[n % RING].at(16 * (n // RING + 1)))
                    for u in (2 * n, 2 * n + 1):
                        if u >= PARTS:
                            a.wait_ge(summed.sem, summed.at(u - PARTS + 1))
                        a.activation(w_hi[:, u % PARTS], half(u), ACT.Copy).then_inc(split_hi.sem, 1)
                    if n >= 3:
                        store(n - 3)
                for n in range(N - 3, N):
                    store(n)
                for s in range(2):
                    a.wait_ge(stored[s].sem, stored[s].at(16 * N // 2))

            @block.tensor
            def _(pe):
                pe.wait_ge(cond_ready.sem, cond_ready.at(3))
                for n in range(N):
                    if n >= 2:
                        pe.wait_ge(drained.sem, drained.at(n - 1))
                    for u in (2 * n, 2 * n + 1):
                        pe.wait_ge(split_lo.sem, split_lo.at(u + 1))
                        for b in range(HJ):
                            j = (u % 2) * HJ + b
                            pe.matmul(acc[:, n % 2, :], a_hi[:, j, :], columns(w_hi, u, b), start=j == 0, stop=False)
                            pe.matmul(acc[:, n % 2, :], a_hi[:, j, :], columns(w_lo, u, b), start=False, stop=False)
                            mm = pe.matmul(acc[:, n % 2, :], a_lo[:, j, :], columns(w_hi, u, b), start=False, stop=j == J - 1)
                        mm.then_inc(summed.sem, 1)

            @block.vector
            def _(dve):
                def drain(n):
                    dve.wait_ge(summed.sem, summed.at(2 * n + 2))
                    if n >= 2:
                        dve.wait_ge(stored[n % 2].sem, stored[n % 2].at(16 * (n // 2)))
                    dve.tensor_tensor(row[:, n % 2, :], acc[0:2, n % 2, :], bias[:, n * CH:(n + 1) * CH], ALU.add).then_inc(drained.sem, 1)

                dve.wait_ge(cond_ready.sem, cond_ready.at(2))
                dve.tensor_tensor(a_lo[:, :, 0:2], act[:], a_hi[:, :, 0:2], ALU.subtract).then_inc(cond_ready.sem, 1)
                dve.wait_ge(also.sem, also.at(32))
                for n in range(N):
                    for u in (2 * n, 2 * n + 1):
                        dve.wait_ge(split_hi.sem, split_hi.at(u + 1))
                        dve.tensor_tensor(w_lo[:, u % PARTS], half(u), w_hi[:, u % PARTS], ALU.subtract).then_inc(split_lo.sem, 1)
                    if n:
                        drain(n - 1)
                drain(N - 1)
        loaded.base += 32
        also.base += 32
        moved.base += 16 * (NT + 1)
        cleared.base += 2
        cond_ready.base += 3
        split_hi.base += 2 * N
        split_lo.base += 2 * N
        for s in range(RING):
            landed[s].base += 16 * (N // RING)
        summed.base += 2 * N
        drained.base += N
        for s in range(2):
            stored[s].base += 16 * N // 2



class Norm:

    def __init__(self, K, ctx, layer, which, bank, store=None):
        self.K, self.layer, self.which, self.bank, self.store = K, layer, which, bank, store
        self.split = store is None
        self.ring = NT if store is not None else 2
        self.gain = K.sb(ctx, "norm_gain", [P, 2, D])
        self.shift = K.sb(ctx, "norm_shift", [P, 2, D])
        self.g = K.sb(ctx, "norm_g", [P, D])
        self.h = K.sb(ctx, "norm_h", [P, self.ring, D])
        self.junk = K.sb(ctx, "norm_squares", [P, D])
        self.ss = K.sb(ctx, "norm_ss", [P, 3, NT])
        self.loaded, self.gained, self.square = K.sig("norm_loaded"), K.sig("norm_gain"), K.sig("norm_square")
        self.mean, self.rstd, self.scaled, self.ready = K.sig("norm_mean"), K.sig("norm_rstd"), K.sig("norm_scaled"), K.sig("norm_h")
        self.turned, self.hi, self.lo = K.sig("norm_turned"), K.sig("norm_hi"), K.sig("norm_lo")
        self.stored = K.sig("norm_stored")

    def load(self, sp):
        K, l = self.K, self.layer
        g = K.I["norm1_g" if self.which == 0 else "norm2_g"][l:l + 1, :]
        sp.dma_start(self.g[:], g.broadcast_to([P, D])).then_inc(self.loaded.sem, 16)
        for cond in range(2):
            at = (l * 6 + 3 * self.which) * D
            sp.dma_start(self.shift[:, cond, :], K.mods[cond:cond + 1, at:at + D].broadcast_to([P, D])).then_inc(self.loaded.sem, 16)
            sp.dma_start(self.gain[:, cond, :], K.mods[cond:cond + 1, at + D:at + 2 * D].broadcast_to([P, D])).then_inc(self.loaded.sem, 16)

    def squares(self, a):
        for t in range(NT):
            a.activation(self.junk[:], self.K.x[:, t, :], ACT.Square, accum_out=self.ss[:, 0, t:t + 1]).then_inc(self.square.sem, 1)
            if t < NT - 1:
                a.wait_ge(self.square.sem, self.square.at(t + 1))

    def rstds(self, pool):
        pool.wait_ge(self.square.sem, self.square.at(NT))
        pool.tensor_scalar(self.ss[:, 1, :], self.ss[:, 0, :], 1.0 / D, EPS, ALU.mult, ALU.add).then_inc(self.mean.sem, 1)
        pool.wait_ge(self.mean.sem, self.mean.at(1))
        pool.tensor_tensor(self.ss[:, 2, :], self.ss[:, 1, :], self.K.minus_half[:].broadcast_to([P, NT]), ALU.pow).then_inc(self.rstd.sem, 1)

    def rows(self, dve):
        K = self.K
        dve.wait_ge(self.loaded.sem, self.loaded.at(80))
        for cond in range(2):
            dve.scalar_tensor_tensor(self.gain[:, cond, :], self.gain[:, cond, :], 1.0, self.g[:], ALU.add, ALU.mult).then_inc(self.gained.sem, 1)
        dve.wait_ge(self.gained.sem, self.gained.at(2))
        dve.wait_ge(self.rstd.sem, self.rstd.at(1))
        for t in range(NT):
            if t >= self.ring:
                dve.wait_ge(self.turned.sem, self.turned.at(2 * (t - 1)))
            cond = 1 if t else 0
            h = self.h[:, t % self.ring, :]
            dve.scalar_tensor_tensor(h, K.x[:, t, :], self.ss[:, 2, t:t + 1], self.gain[:, cond, :], ALU.mult, ALU.mult).then_inc(self.scaled.sem, 1)
            dve.wait_ge(self.scaled.sem, self.scaled.at(t + 1))
            dve.tensor_tensor(h, h, self.shift[:, cond, :], ALU.add).then_inc(self.ready.sem, 1)
            if t >= 1 and self.split:
                self.part_lo(dve, t - 1)
        if self.split:
            self.part_lo(dve, NT - 1)

    def part_lo(self, dve, t):
        for half in range(2):
            n = 2 * t + half
            dve.wait_ge(self.hi.sem, self.hi.at(n + 1))
            at = (slice(None), slice(4 * half, 4 * half + 4), slice(t * P, (t + 1) * P))
            dve.tensor_tensor(self.K.h_lo[at], self.bank[:, n % 2, :].rearrange("p (j n) -> p j n", j=4),
                              self.K.h_hi[at], ALU.subtract).then_inc(self.lo.sem, 1)

    def turn(self, pe):
        for t in range(NT):
            pe.wait_ge(self.ready.sem, self.ready.at(t + 1))
            for half in range(2):
                n = 2 * t + half
                if n >= 2:
                    pe.wait_ge(self.lo.sem, self.lo.at(n - 1))
                for j in range(4):
                    mm = pe.transpose(self.bank[:, n % 2, j * P:(j + 1) * P],
                                      self.h[:, t % self.ring, 4 * half + j:D:J], self.K.ident[:])
                mm.then_inc(self.turned.sem, 1)
        pe.wait_ge(self.lo.sem, self.lo.at(2 * NT))

    def parts_hi(self, a):
        for n in range(2 * NT):
            a.wait_ge(self.turned.sem, self.turned.at(n + 1))
            t, half = divmod(n, 2)
            a.activation(self.K.h_hi[:, 4 * half:4 * half + 4, t * P:(t + 1) * P],
                         self.bank[:, n % 2, :].rearrange("p (j n) -> p j n", j=4), ACT.Copy).then_inc(self.hi.sem, 1)

    def store_rows(self, sp):
        for t in range(NT):
            sp.wait_ge(self.ready.sem, self.ready.at(t + 1))
            sp.dma_start(self.store[t * P:(t + 1) * P, :], self.h[:, t % self.ring, :]).then_inc(self.stored.sem, 16)
        sp.wait_ge(self.stored.sem, self.stored.at(16 * NT))

    def end(self):
        self.loaded.base += 80
        self.gained.base += 2
        self.square.base += NT
        self.mean.base += 1
        self.rstd.base += 1
        self.scaled.base += NT
        self.ready.base += NT
        self.turned.base += 2 * NT
        if self.split:
            self.hi.base += 2 * NT
            self.lo.base += 2 * NT
        else:
            self.stored.base += 16 * NT



class Turn:

    def __init__(self, K, rows, blocks, first, bank, flip=None):
        self.K, self.rows, self.blocks, self.first, self.bank, self.flip = K, rows, blocks, first, bank, flip
        self.groups = [(t, g) for t in range(NT) for g in range(0, blocks, 4)]
        self.done, self.hi, self.lo = K.sig("turn_done"), K.sig("turn_hi"), K.sig("turn_lo")

    def turn(self, pe):
        for n, (t, g) in enumerate(self.groups):
            if n >= 2:
                pe.wait_ge(self.lo.sem, self.lo.at(n - 1))
            for b in range(4):
                out = self.bank[:, n % 2, b * P:(b + 1) * P]
                if self.flip is None:
                    mm = pe.transpose(out, self.rows(t, g + b), self.K.ident[:])
                else:
                    mm = pe.matmul(out, self.rows(t, g + b), self.flip[:], start=True, stop=True)
            mm.then_inc(self.done.sem, 1)

    def out(self, h, t, g):
        return h[:, self.first + g:self.first + g + 4, t * P:(t + 1) * P]

    def parts_hi(self, a):
        for n, (t, g) in enumerate(self.groups):
            a.wait_ge(self.done.sem, self.done.at(n + 1))
            a.activation(self.out(self.K.h_hi, t, g), self.bank[:, n % 2, :].rearrange("p (j n) -> p j n", j=4),
                         ACT.Copy).then_inc(self.hi.sem, 1)

    def parts_lo(self, dve):
        for n, (t, g) in enumerate(self.groups):
            dve.wait_ge(self.hi.sem, self.hi.at(n + 1))
            dve.tensor_tensor(self.out(self.K.h_lo, t, g), self.bank[:, n % 2, :].rearrange("p (j n) -> p j n", j=4),
                              self.out(self.K.h_hi, t, g), ALU.subtract).then_inc(self.lo.sem, 1)

    def end(self):
        for s in (self.done, self.hi, self.lo):
            s.base += len(self.groups)



def project_stage(K, layer, w, chunks, width, z, together):
    if not together:
        norm_stage(K, layer, 0)
    with ExitStack() as ctx:
        norm = Norm(K, ctx, layer, 0, K.ps(ctx, "norm_bank", [P, 2, 512])) if together else None
        w = rows_by_partition(w)
        g = Gemm(K, ctx, chunks, 4, width,
                 lambda c, k: [(slice(0, width), w[:, 2 * k:2 * k + 2, bass.ds(c * width, width)])],
                 lambda j, t: K.h_hi[:, j, t * P:(t + 1) * P], lambda j, t: K.h_lo[:, j, t * P:(t + 1) * P])
        with K.nc.Block() as block:
            @block.sync
            def _(sp):
                if together:
                    norm.load(sp)
                g.each_unit(sp, g.load)

            @block.gpsimd
            def _(pool):
                if together:
                    norm.rstds(pool)

            @block.tensor
            def _(pe):
                if together:
                    norm.turn(pe)
                g.each_unit(pe, g.products)

            @block.scalar
            def _(a):
                if together:
                    norm.squares(a)
                    norm.parts_hi(a)

                def drain(c):
                    for t in range(NT):
                        g.wait_sum(a, c, t)
                        a.activation(z[:, t, bass.ds(c * width, width)], g.acc[:, t, 0:width], ACT.Copy).then_inc(g.drained.sem, 1)
                g.each_unit(a, g.split_hi, {0: drain})

            @block.vector
            def _(dve):
                if together:
                    norm.rows(dve)
                g.each_unit(dve, g.split_lo)
        g.end()
        if together:
            norm.end()


def output_stage(K, layer, gate_row, w, rows, units, turn=None, hi=None, lo=None):
    nc = K.nc
    with ExitStack() as ctx:
        gate = K.sb(ctx, "gate", [P, 2, D])
        tmp = K.sb(ctx, "gated", [P, 2, 512])
        w = rows(w)
        g = Gemm(K, ctx, 2, units, 512,
                 lambda c, k: [(slice(0, 512), w[:, 2 * k:2 * k + 2, c * 512:(c + 1) * 512])], hi, lo)
        loaded, gated, added = K.sig("also_loaded"), K.sig("gated"), K.sig("x_added")
        with nc.Block() as block:
            @block.sync
            def _(sp):
                for cond in range(2):
                    at = (layer * 6 + gate_row) * D
                    sp.dma_start(gate[:, cond, :], K.mods[cond:cond + 1, at:at + D].broadcast_to([P, D])).then_inc(loaded.sem, 16)
                g.each_unit(sp, g.load)

            @block.tensor
            def _(pe):
                if turn is not None:
                    turn.turn(pe)
                    pe.wait_ge(turn.lo.sem, turn.lo.at(len(turn.groups)))
                g.each_unit(pe, g.products)

            @block.scalar
            def _(a):
                if turn is not None:
                    turn.parts_hi(a)
                g.each_unit(a, g.split_hi)

            @block.vector
            def _(dve):
                if turn is not None:
                    turn.parts_lo(dve)
                dve.wait_ge(loaded.sem, loaded.at(32))

                def drain(c):
                    for t in range(NT):
                        n = c * NT + t
                        g.wait_sum(dve, c, t)
                        if n >= 2:
                            dve.wait_ge(added.sem, added.at(n - 1))
                        dve.tensor_tensor(tmp[:, n % 2, :], g.acc[:, t, :], gate[:, 1 if t else 0, c * 512:(c + 1) * 512],
                                          ALU.mult).then_inc(g.drained.sem, 1)
                g.each_unit(dve, g.split_lo, {0: drain})

            @block.gpsimd
            def _(pool):
                for c in range(2):
                    for t in range(NT):
                        pool.wait_ge(g.drained.sem, g.drained.at(c * NT + t + 1))
                        x = K.x[:, t, c * 512:(c + 1) * 512]
                        pool.tensor_tensor(x, x, tmp[:, (c * NT + t) % 2, :], ALU.add).then_inc(added.sem, 1)
        g.end()
        loaded.base += 32
        added.base += 2 * NT
        if turn is not None:
            turn.end()


def norm_stage(K, layer, which):
    with ExitStack() as ctx:
        bank = K.ps(ctx, "norm_bank", [P, 2, 512])
        norm = Norm(K, ctx, layer, which, bank)
        with K.nc.Block() as block:
            @block.sync
            def _(sp):
                norm.load(sp)

            @block.gpsimd
            def _(pool):
                norm.rstds(pool)

            @block.tensor
            def _(pe):
                norm.turn(pe)

            @block.scalar
            def _(a):
                norm.squares(a)
                norm.parts_hi(a)

            @block.vector
            def _(dve):
                norm.rows(dve)
        norm.end()


def ffn_stage(K):
    HALF, NB = 256, D_FF // P
    with ExitStack() as outer:
        a_hi = K.sb(outer, "a_hi", [P, NB, T], F32R)
        a_lo = K.sb(outer, "a_lo", [P, NB, T], F32R)
        with ExitStack() as ctx:
            K.transposed_rows(ctx)
            norm_stage(K, 0, 1)
            bank = K.ps(ctx, "turn_bank", [P, 3, 2, HALF])
            act = K.sb(ctx, "act", [P, NT, HALF])
            wp = rows_by_partition(K.I["ffn_w_gu"][0])
            g = Gemm(K, ctx, D_FF // HALF, 4, 512,
                     lambda c, k: [(slice(h * HALF, (h + 1) * HALF),
                                    wp[:, 2 * k:2 * k + 2, bass.ds(c * HALF + h * D_FF, HALF)]) for h in range(2)],
                     lambda j, t: K.h_hi[:, j, t * P:(t + 1) * P], lambda j, t: K.h_lo[:, j, t * P:(t + 1) * P], parts=2)
            s_silu, s_turned, s_hi, s_lo = K.sig("ffn_silu"), K.sig("ffn_turned"), K.sig("ffn_hi"), K.sig("ffn_lo")

            def turned(t):
                return bank[:, t % 3, t // 3, :].rearrange("p (j n) -> p j n", j=2)

            def place(a, c, t):
                return a[:, bass.ds(c * 2, 2), t * P:(t + 1) * P]

            with K.nc.Block() as block:
                @block.sync
                def _(sp):
                    g.each_unit(sp, g.load)

                @block.tensor
                def _(pe):
                    def turns(c):
                        for t in range(NT):
                            pe.wait_ge(g.drained.sem, g.drained.at(c * NT + (t + 1)))
                            if t == 0:
                                pe.wait_ge(s_lo.sem, s_lo.at(c * NT))
                            for b in range(2):
                                mm = pe.transpose(bank[:, t % 3, t // 3, b * P:(b + 1) * P], act[:, t, b * P:(b + 1) * P], K.ident[:])
                            mm.then_inc(s_turned.sem, 1)
                    g.each_unit(pe, g.products, {0: turns})

                @block.scalar
                def _(a):
                    def gates(c):
                        for t in range(NT):
                            g.wait_sum(a, c, t)
                            if t == 0:
                                a.wait_ge(s_turned.sem, s_turned.at(c * NT))
                            a.activation(act[:, t, :], g.acc[:, t, 0:HALF], ACT.Silu).then_inc(s_silu.sem, 1)

                    def parts(c):
                        for t in range(NT):
                            a.wait_ge(s_turned.sem, s_turned.at(c * NT + min(t + 4, NT)))
                            if t >= 3:
                                a.wait_ge(s_lo.sem, s_lo.at(c * NT + (t - 2)))
                            a.activation(place(a_hi, c, t), turned(t), ACT.Copy).then_inc(s_hi.sem, 1)
                    g.each_unit(a, g.split_hi, {0: gates, 1: parts})

                @block.vector
                def _(dve):
                    def ups(c):
                        for t in range(NT):
                            dve.wait_ge(s_silu.sem, s_silu.at(c * NT + (t + 1)))
                            dve.tensor_tensor(act[:, t, :], act[:, t, :], g.acc[:, t, HALF:2 * HALF],
                                              ALU.mult).then_inc(g.drained.sem, 1)

                    def parts(c):
                        for t in range(NT):
                            dve.wait_ge(s_hi.sem, s_hi.at(c * NT + (t + 1)))
                            dve.tensor_tensor(place(a_lo, c, t), turned(t), place(a_hi, c, t), ALU.subtract).then_inc(s_lo.sem, 1)
                    g.each_unit(dve, g.split_lo, {0: ups, 1: parts})
            g.end()
            for s in (s_silu, s_turned, s_hi, s_lo):
                s.base += g.chunks * NT
        output_stage(K, 0, 5, K.I["ffn_w_dn"][0], rows_by_block, NB // 2,
                     hi=lambda j, t: a_hi[:, j, t * P:(t + 1) * P], lo=lambda j, t: a_lo[:, j, t * P:(t + 1) * P])



def shift_stage(K, z, zs):
    with ExitStack() as ctx:
        W = T + 3
        pad = K.sb(ctx, "padded", [P, 3, W])
        mid = K.sb(ctx, "neighbours", [P, 3, W])
        mu = K.sb(ctx, "mu", [P, ZT])
        bank = K.ps(ctx, "shift_bank", [P, 2, 1024])
        loaded, cleared = K.sig("loaded"), K.sig("shift_cleared")
        s_turned, s_pad, s_sum, s_half, s_mixed = (K.sig("shift_" + n) for n in ("turned", "padded", "sum", "half", "mixed"))
        with K.nc.Block() as block:
            @block.sync
            def _(sp):
                with K.nc.allow_non_contiguous_dma("1920 mixing weights, one to a channel"):
                    sp.dma_start(mu[:], K.I["b_mu"][0].rearrange("(c p) -> p c", p=P)).then_inc(loaded.sem, 16)

            @block.tensor
            def _(pe):
                for c in range(ZT):
                    if c >= 2:
                        pe.wait_ge(s_pad.sem, s_pad.at(2 * (c - 1)))
                    for t in range(NT):
                        mm = pe.transpose(bank[:, c % 2, t * P:(t + 1) * P], z[:, t, QKV_E + c * P:QKV_E + (c + 1) * P], K.ident[:])
                    mm.then_inc(s_turned.sem, 1)

            @block.scalar
            def _(a):
                a.wait_ge(cleared.sem, cleared.at(1))
                for c in range(ZT):
                    a.wait_ge(s_turned.sem, s_turned.at(c + 1))
                    if c >= 3:
                        a.wait_ge(s_mixed.sem, s_mixed.at(2 * (c - 2)))
                    a.activation(pad[:, c % 3, 1:P + 1], bank[:, c % 2, 0:P], ACT.Copy).then_inc(s_pad.sem, 1)
                    a.activation(pad[:, c % 3, P + 2:T + 2], bank[:, c % 2, P:T], ACT.Copy).then_inc(s_pad.sem, 1)

            @block.gpsimd
            def _(pool):
                pool.memset(pad[:], 0.0).then_inc(cleared.sem, 1)
                for c in range(ZT):
                    pool.wait_ge(s_pad.sem, s_pad.at(2 * (c + 1)))
                    if c >= 3:
                        pool.wait_ge(s_mixed.sem, s_mixed.at(2 * (c - 2)))
                    pool.tensor_tensor(mid[:, c % 3, 1:W - 1], pad[:, c % 3, 0:W - 2], pad[:, c % 3, 2:W], ALU.add).then_inc(s_sum.sem, 1)

            @block.vector
            def _(dve):
                dve.wait_ge(loaded.sem, loaded.at(16))
                for c in range(ZT):
                    dve.wait_ge(s_sum.sem, s_sum.at(c + 1))
                    m, z0 = mid[:, c % 3], pad[:, c % 3]
                    dve.scalar_tensor_tensor(m[:, 1:W - 1], m[:, 1:W - 1], 0.5, z0[:, 1:W - 1], ALU.mult, ALU.subtract).then_inc(s_half.sem, 1)
                    dve.wait_ge(s_half.sem, s_half.at(c + 1))
                    for at, to, n in ((1, 0, P), (P + 2, P, T - P)):
                        dve.scalar_tensor_tensor(zs[:, c, to:to + n], m[:, at:at + n], mu[:, c:c + 1], z0[:, at:at + n],
                                                 ALU.mult, ALU.add).then_inc(s_mixed.sem, 1)
        loaded.base += 16
        cleared.base += 1
        for s, n in ((s_turned, 1), (s_pad, 2), (s_sum, 1), (s_half, 1), (s_mixed, 2)):
            s.base += n * ZT



class Attention:

    PIECES = ((0, 4, 0), (0, 5, 4), (1, 4, 0), (1, 7, 4))

    def __init__(self, K, ctx, heads, items, biased, bias_ready=None, flip=None):
        self.bias_ready, self.flip = bias_ready, flip
        self.K, self.heads, self.items, self.biased = K, heads, items, biased
        self.s = K.ps(ctx, "scores", [P, 2, 1024])
        self.pt = K.ps(ctx, "probs_turned", [P, 1024])
        self.o = K.ps(ctx, "att_out", [P, 512])
        self.bank = K.ps(ctx, "att_pieces", [P, 512])
        self.q = K.sb(ctx, "q_stack", [P, 2, NT * P], F32R)
        self.k = K.sb(ctx, "k_stack", [P, 2, 2, (NT + 2) * P], F32R)
        self.rows = [K.sb(ctx, f"rows_doubled{r}", [P, (to - first) * P]) for r, (_, to, first) in enumerate(self.PIECES)]
        self.copies, self.doubled, self.copied_rows = K.sig("qk_sums"), K.sig("qk_square"), 0
        self.p = K.sb(ctx, "probs", [P, 3, 768])
        self.ptb = K.sb(ctx, "probs_t", [P, 2, 768])
        self.stat = K.sb(ctx, "att_stat", [P, 4, 4])
        if biased:
            self.sb = K.sb(ctx, "scores_biased", [P, 2, 768])
        names = ("piece", "piece_hi", "piece_lo", "scores", "biased", "max", "exp", "turned", "probs", "values", "sum", "out")
        (self.pieced, self.piece_hi, self.piece_lo, self.scored, self.biasd, self.shifted, self.exped, self.turned, self.copied,
         self.valued, self.summed, self.done) = (K.sig("att_" + n) for n in names)

    def piece_of(self, i):
        h, r = (i + 1) // NT + 1, (i + 1) % NT
        return (h, r) if 0 <= i and h < len(self.heads) and r < len(self.PIECES) else None

    def piece_pe(self, pe, h, r):
        n = len(self.PIECES) * h + r
        which, to, first = self.PIECES[r]
        if n:
            pe.wait_ge(self.piece_lo.sem, self.piece_lo.at(n))
        pe.wait_ge(self.doubled.sem, self.doubled.at(n + 1))
        for b in range(first, to):
            rows = self.rows[r][:, (b - first) * P:(b - first + 1) * P]
            out = self.bank[:, (b - first) * P:(b - first + 1) * P]
            if which == 0 and self.flip is not None:
                mm = pe.matmul(out, rows, self.flip[:], start=True, stop=True)
            else:
                mm = pe.transpose(out, rows, self.K.ident[:])
        mm.then_inc(self.pieced.sem, 1)

    def double(self, pool, h, r):
        n = len(self.PIECES) * h + r
        which, to, first = self.PIECES[r]
        if h:
            pool.wait_ge(self.pieced.sem, self.pieced.at(n - len(self.PIECES) + 1))
        tiles, at = to - first, 0
        for src, m in self.heads[h]["qk"[which]]:
            x, y = max(first, at), min(to, at + m)
            if x < y:
                out = self.rows[r][:, (x - first) * P:(y - first) * P].rearrange("p (t o d) -> p t o d", o=2, d=HD)
                for o in range(2):
                    ins = pool.tensor_copy(out[:, :, o, :], src[:, x - at:y - at, :])
                    ins.then_inc(self.copies.sem, 1)
                    self.copied_rows += 1
            at += m
        pool.wait_ge(self.copies.sem, self.copies.at(self.copied_rows))
        pool.sem_inc(self.doubled.sem, 1)

    def piece_act(self, a, h, r):
        n = len(self.PIECES) * h + r
        which, to, first = self.PIECES[r]
        cols, w = slice(first * P, to * P), (to - first) * P
        a.wait_ge(self.pieced.sem, self.pieced.at(n + 1))
        out = self.q[:, h % 2, cols] if which == 0 else self.k[:, h % 2, 0, cols]
        a.activation(out, self.bank[:, 0:w], ACT.Copy, scale=(SCALE, 1.0)[which]).then_inc(self.piece_hi.sem, 1)

    def piece_dve(self, dve, h, r):
        n = len(self.PIECES) * h + r
        which, to, first = self.PIECES[r]
        cols, w = slice(first * P, to * P), (to - first) * P
        dve.wait_ge(self.piece_hi.sem, self.piece_hi.at(n + 1))
        if which == 0:
            q = self.q[HD:P, h % 2, cols]
            dve.scalar_tensor_tensor(q, self.bank[HD:P, 0:w], SCALE, q, ALU.mult, ALU.subtract).then_inc(self.piece_lo.sem, 1)
        else:
            dve.tensor_tensor(self.k[:, h % 2, 1, cols], self.bank[:, 0:w], self.k[:, h % 2, 0, cols], ALU.subtract).then_inc(self.piece_lo.sem, 1)

    def first_head(self, eng, piece):
        for r in range(len(self.PIECES)):
            piece(eng, 0, r)
        piece(eng, 1, 0)

    def products(self, pe):
        n = len(self.items)
        self.first_head(pe, self.piece_pe)
        for i in range(n + 3):
            if i < n:
                h, t = divmod(i, NT)
                if t == 0:
                    pe.wait_ge(self.piece_lo.sem, self.piece_lo.at(len(self.PIECES) * (h + 1)))
                if i >= 2:
                    if self.biased:
                        pe.wait_ge(self.biasd.sem, self.biasd.at(2 * (i - 1)))
                    else:
                        pe.wait_ge(self.exped.sem, self.exped.at(i - 1))
                at = 0
                q = self.q[:, h % 2, t * P:(t + 1) * P]
                for x, y in ((0, P),) if t == 0 else ((P, T), (T, T + CACHE)):
                    pe.matmul(self.s[:, i % 2, at:at + y - x], q, self.k[:, h % 2, 0, x:y], start=True, stop=False)
                    mm = pe.matmul(self.s[:, i % 2, at:at + y - x], q, self.k[:, h % 2, 1, x:y], start=False, stop=True)
                    at += y - x
                mm.then_inc(self.scored.sem, 1)
            if 2 <= i < n + 2:
                j = i - 2
                pe.wait_ge(self.exped.sem, self.exped.at(j + 1))
                pe.wait_ge(self.copied.sem, self.copied.at(j))
                for b in range(len(self.items[j]["values"])):
                    mm = pe.transpose(self.pt[:, b * P:(b + 1) * P], self.p[:, j % 3, b * P:(b + 1) * P], self.K.ident[:])
                mm.then_inc(self.turned.sem, 1)
            if i >= 3:
                j = i - 3
                pe.wait_ge(self.copied.sem, self.copied.at(j + 1))
                if j:
                    pe.wait_ge(self.done.sem, self.done.at(j))
                v = self.items[j]["values"]
                for b in range(len(v)):
                    mm = pe.matmul(self.o[:, 0:HD], self.ptb[:, j % 2, b * P:(b + 1) * P], v[b], start=b == 0, stop=b == len(v) - 1)
                mm.then_inc(self.valued.sem, 1)
            if self.piece_of(i) is not None:
                self.piece_pe(pe, *self.piece_of(i))

    def width(self, i):
        return P * len(self.items[i]["values"])

    def exps(self, a):
        n = len(self.items)
        self.first_head(a, self.piece_act)
        for i in range(n + 2):
            if self.piece_of(i - 1) is not None:
                self.piece_act(a, *self.piece_of(i - 1))
            if i >= 2:
                j = i - 2
                w = self.width(j)
                a.wait_ge(self.turned.sem, self.turned.at(j + 1))
                if j >= 2:
                    a.wait_ge(self.valued.sem, self.valued.at(j - 1))
                a.activation(self.ptb[:, j % 2, 0:w], self.pt[:, 0:w], ACT.Copy).then_inc(self.copied.sem, 1)
            if i < n:
                w = self.width(i)
                a.wait_ge(self.shifted.sem, self.shifted.at(i + 1))
                if i >= 3:
                    a.wait_ge(self.turned.sem, self.turned.at(i - 2))
                src = self.sb if self.biased else self.s
                a.activation(self.p[:, i % 3, 0:w], src[:, i % 2, 0:w], ACT.Exp, bias=self.stat[:, i % 4, 0:1],
                             accum_out=self.stat[:, i % 4, 2:3]).then_inc(self.exped.sem, 1)

    def maxima(self, dve):
        n = len(self.items)
        self.first_head(dve, self.piece_dve)
        for i in range(n + 4):
            if i >= 4:
                j = i - 4
                dve.wait_ge(self.exped.sem, self.exped.at(j + 1))
                dve.reciprocal(self.stat[:, j % 4, 3:4], self.stat[:, j % 4, 2:3]).then_inc(self.summed.sem, 1)
                dve.wait_ge(self.summed.sem, self.summed.at(j + 1))
                dve.wait_ge(self.valued.sem, self.valued.at(j + 1))
                dve.tensor_scalar(self.items[j]["out"], self.o[:, 0:HD], self.stat[:, j % 4, 3:4], None,
                                  ALU.mult).then_inc(self.done.sem, 1)
            if i < n:
                it, w = self.items[i], self.width(i)
                dve.wait_ge(self.scored.sem, self.scored.at(i + 1))
                s = self.s[:, i % 2, 0:w]
                if self.biased:
                    if i >= 2:
                        dve.wait_ge(self.exped.sem, self.exped.at(i - 1))
                    sb = self.sb[:, i % 2]
                    if it["bias"] is None:
                        dve.tensor_copy(sb[:, 0:w], s).then_inc(self.biasd.sem, 2)
                    else:
                        dve.wait_ge(self.bias_ready.sem, self.bias_ready.at(it["head"] + 1))
                        dve.tensor_tensor(sb[:, 0:512], s[:, 0:512], it["bias"], ALU.add).then_inc(self.biasd.sem, 1)
                        dve.tensor_copy(sb[:, 512:w], s[:, 512:w]).then_inc(self.biasd.sem, 1)
                    dve.wait_ge(self.biasd.sem, self.biasd.at(2 * i + 2))
                    s = sb[:, 0:w]
                    if self.piece_of(i - 1) is not None:
                        self.piece_dve(dve, *self.piece_of(i - 1))
                dve.tensor_reduce(self.stat[:, i % 4, 0:1], s, AX.X, ALU.max, negate=True).then_inc(self.shifted.sem, 1)
                if not self.biased and self.piece_of(i - 1) is not None:
                    self.piece_dve(dve, *self.piece_of(i - 1))

    def end(self):
        n = len(self.items)
        self.copies.base += self.copied_rows
        for s in (self.doubled, self.pieced, self.piece_hi, self.piece_lo):
            s.base += len(self.PIECES) * len(self.heads)
        for s in (self.scored, self.shifted, self.exped, self.turned, self.copied, self.valued, self.summed, self.done):
            s.base += n
        if self.biased:
            self.biasd.base += 2 * n


def even_attention_stage(K, z):
    I, O = K.I, K.O
    NH = A_HEADS + A_KV
    with ExitStack() as ctx:
        kc, vc = (K.sb(ctx, n, [P, 2, A_KV * HD]) for n in ("k_cache", "v_cache"))
        loaded = K.sig("loaded")
        names = ("square", "sums", "mean", "rstd", "normed", "gained", "cos", "sin", "roped", "stored")
        (s_square, s_sums, s_mean, s_rstd, s_normed, s_gained, s_cos, s_sin, s_roped, s_stored) = (
            K.sig("qk_" + n) for n in names)
        with ExitStack() as prep:
            gain = K.sb(prep, "qk_gain", [P, NH, HD])
            rope = K.sb(prep, "rope", [P, NT - 1, 2, HD])
            sq = K.sb(prep, "qk_square", [P, 2, NH * HD])
            ss = K.sb(prep, "qk_ss", [P, 3, NT, NH])
            t2 = K.sb(prep, "qk_sin", [P, 2, NH, HD])

            def heads(t):
                return z[:, t, 0:NH * HD].rearrange("p (h d) -> p h d", h=NH)

            with K.nc.Block() as block:
                @block.sync
                def _(sp):
                    sp.dma_start(rope[:], I["const_rope"]).then_inc(loaded.sem, 16)
                    for h in range(NH):
                        g = I["a_q_gain" if h < A_HEADS else "a_k_gain"]
                        sp.dma_start(gain[:, h, :], g.broadcast_to([P, HD])).then_inc(loaded.sem, 16)
                    for t in range(2):
                        sp.dma_start(kc[:, t, :], I["cache_a_k"][0, 0, t * P:(t + 1) * P].rearrange("p h d -> p (h d)")).then_inc(loaded.sem, 16)
                        sp.dma_start(vc[:, t, :], I["cache_a_v"][0, 0, t * P:(t + 1) * P].rearrange("p h d -> p (h d)")).then_inc(loaded.sem, 16)
                    sp.wait_ge(s_gained.sem, s_gained.at(1))
                    sp.dma_start(O["new_cache_a_k"][0, 0].rearrange("t h d -> t (h d)"), z[:, 0, 512:640]).then_inc(s_stored.sem, 16)
                    sp.dma_start(O["new_cache_a_v"][0, 0].rearrange("t h d -> t (h d)"), z[:, 0, 640:768]).then_inc(s_stored.sem, 16)
                    sp.wait_ge(s_stored.sem, s_stored.at(32))

                @block.scalar
                def _(a):
                    for t in range(NT):
                        if t >= 2:
                            a.wait_ge(s_sums.sem, s_sums.at(t - 1))
                        a.activation(sq[:, t % 2, :], z[:, t, 0:NH * HD], ACT.Square).then_inc(s_square.sem, 1)

                @block.gpsimd
                def _(pool):
                    pool.wait_ge(s_sums.sem, s_sums.at(NT))
                    pool.tensor_scalar(ss[:, 1], ss[:, 0], 1.0 / HD, EPS, ALU.mult, ALU.add).then_inc(s_mean.sem, 1)
                    pool.wait_ge(s_mean.sem, s_mean.at(1))
                    pool.tensor_tensor(ss[:, 2].rearrange("p t h -> p (t h)"), ss[:, 1].rearrange("p t h -> p (t h)"),
                                       K.minus_half[:].broadcast_to([P, NT * NH]), ALU.pow).then_inc(s_rstd.sem, 1)
                    for t in range(1, NT):
                        pool.wait_ge(s_sin.sem, s_sin.at(2 * t))
                        c = rope[:, t - 1, 0:1, :].broadcast_to([P, NH, HD])
                        pool.tensor_tensor(heads(t), heads(t), c, ALU.mult).then_inc(s_cos.sem, 1)
                        pool.wait_ge(s_cos.sem, s_cos.at(t))
                        pool.tensor_tensor(heads(t), heads(t), t2[:, t % 2], ALU.add).then_inc(s_roped.sem, 1)

                @block.vector
                def _(dve):
                    for t in range(NT):
                        dve.wait_ge(s_square.sem, s_square.at(t + 1))
                        dve.tensor_reduce(ss[:, 0, t, :], sq[:, t % 2, :].rearrange("p (h d) -> p h d", h=NH), AX.X, ALU.add).then_inc(s_sums.sem, 1)
                    dve.wait_ge(s_rstd.sem, s_rstd.at(1))
                    dve.wait_ge(loaded.sem, loaded.at(16 * (1 + NH + 4)))
                    for t in range(NT):
                        r = ss[:, 2, t, :].rearrange("p (h o) -> p h o", o=1).broadcast_to([P, NH, HD])
                        dve.tensor_tensor(heads(t), heads(t), r, ALU.mult).then_inc(s_normed.sem, 1)
                        dve.wait_ge(s_normed.sem, s_normed.at(t + 1))
                        dve.tensor_tensor(heads(t), heads(t), gain[:], ALU.mult).then_inc(s_gained.sem, 1)
                        if t == 0:
                            continue
                        dve.wait_ge(s_gained.sem, s_gained.at(t + 1))
                        if t >= 3:
                            dve.wait_ge(s_roped.sem, s_roped.at(t - 2))
                        x = z[:, t, 0:NH * HD].rearrange("p (h two d) -> p h two d", two=4, d=16)
                        out = t2[:, t % 2].rearrange("p h (two d) -> p h two d", two=4)
                        s = rope[:, t - 1, 1, :].rearrange("p (o two d) -> p o two d", o=1, two=4)
                        for a, b in ((0, 1), (1, 0)):
                            dve.tensor_tensor(out[:, :, a::2, :], x[:, :, b::2, :], s[:, :, a::2, :].broadcast_to([P, NH, 2, 16]),
                                              ALU.mult).then_inc(s_sin.sem, 1)
            loaded.base += 16 * (1 + NH + 4)
            s_stored.base += 32
            for s, n in ((s_square, NT), (s_sums, NT), (s_mean, 1), (s_rstd, 1), (s_normed, NT), (s_gained, NT), (s_cos, NT - 1),
                         (s_sin, 2 * (NT - 1)), (s_roped, NT - 1)):
                s.base += n

        with ExitStack() as att:
            heads, items = [], []
            for h in range(A_HEADS):
                g = h // (A_HEADS // A_KV)
                heads.append({"q": [(z[:, :, h * HD:(h + 1) * HD], NT)],
                              "k": [(z[:, :, 512 + g * HD:512 + (g + 1) * HD], NT), (kc[:, :, g * HD:(g + 1) * HD], 2)]})
                vcols = slice(640 + g * HD, 640 + (g + 1) * HD)
                for t in range(NT):
                    values = [z[:, 0, vcols]]
                    if t:
                        values = [z[:, u, vcols] for u in range(1, NT)] + [vc[:, u, g * HD:(g + 1) * HD] for u in range(2)]
                    items.append({"values": values, "out": z[:, t, h * HD:(h + 1) * HD]})
            at = Attention(K, att, heads, items, biased=False)
            attention_block(K, at)
        turn_block(K, lambda t, b: z[:, t, b * P:(b + 1) * P], 4, 0)


def attention_block(K, at, sync=None, gpsimd=None):
    with K.nc.Block() as block:
        if sync is not None:
            @block.sync
            def _(sp):
                sync(sp)

        @block.gpsimd
        def _(pool):
            for h in range(len(at.heads)):
                for r in range(len(at.PIECES)):
                    at.double(pool, h, r)
                if gpsimd is not None:
                    gpsimd(pool, h)

        @block.tensor
        def _(pe):
            at.products(pe)

        @block.scalar
        def _(a):
            at.exps(a)

        @block.vector
        def _(dve):
            at.maxima(dve)
    at.end()


def turn_block(K, rows, blocks, first):
    with ExitStack() as ctx:
        turn = Turn(K, rows, blocks, first, K.ps(ctx, "turn_bank", [P, 2, 512]))
        with K.nc.Block() as block:
            @block.tensor
            def _(pe):
                turn.turn(pe)

            @block.scalar
            def _(a):
                turn.parts_hi(a)

            @block.vector
            def _(dve):
                turn.parts_lo(dve)
        turn.end()


def odd_attention_stage(K, z, flip):
    I, O = K.I, K.O
    DR = 14
    with ExitStack() as ctx:
        kc, vc = (K.sb(ctx, n, [P, 2, D]) for n in ("k_cache", "v_cache"))
        loaded, s_stored, s_zero = K.sig("loaded"), K.sig("qk_stored"), K.sig("rpb_zero")
        s_rpb, s_flip = K.sig("rpb_stored"), K.sig("also_loaded")
        with ExitStack() as prep:
            pad = K.sb(prep, "rpb_padded", [120, 2, P])
            with K.nc.Block() as block:
                @block.gpsimd
                def _(pool):
                    pool.memset(pad[:], 0.0).then_inc(s_zero.sem, 1)

                @block.sync
                def _(sp):
                    sp.dma_start(flip[:], I["const_flip"]).then_inc(s_flip.sem, 16)
                    for t in range(2):
                        sp.dma_start(kc[:, t, :], I["cache_c_k"][0, 0, t * P:(t + 1) * P].rearrange("p h d -> p (h d)")).then_inc(loaded.sem, 16)
                        sp.dma_start(vc[:, t, :], I["cache_c_v"][0, 0, t * P:(t + 1) * P].rearrange("p h d -> p (h d)")).then_inc(loaded.sem, 16)
                    sp.dma_start(O["new_cache_c_k"][0, 0].rearrange("t h d -> t (h d)"), z[:, 0, D:2 * D]).then_inc(s_stored.sem, 16)
                    sp.dma_start(O["new_cache_c_v"][0, 0].rearrange("t h d -> t (h d)"), z[:, 0, 2 * D:3 * D]).then_inc(s_stored.sem, 16)
                    sp.wait_ge(s_zero.sem, s_zero.at(1))
                    rpb = I["c_rpb"][0].rearrange("h r c -> (h r) c").rearrange("(a p) c -> p a c", a=2)
                    sp.dma_start(pad[:, :, 48:79], rpb).then_inc(loaded.sem, 16)
                    sp.wait_ge(loaded.sem, loaded.at(80))
                    sp.dma_start(K.rpb_rows.rearrange("(a p) c -> p a c", a=2), pad[:]).then_inc(s_rpb.sem, 16)
                    sp.wait_ge(s_rpb.sem, s_rpb.at(16))
                    sp.wait_ge(s_stored.sem, s_stored.at(32))
                    sp.wait_ge(s_flip.sem, s_flip.at(16))
            loaded.base += 80
            s_stored.base += 32
            s_rpb.base += 16
            s_flip.base += 16
            s_zero.base += 1

        with ExitStack() as att:
            NB = 2
            bias = K.sb(att, "bias", [P, NB, DR, HD])
            outside = K.sb(att, "outside", [P, HD])
            s_masked, landed = K.sig("bias_masked"), [K.sig(f"bias_landed{s}") for s in range(NB)]
            heads, items = [], []
            for h in range(C_HEADS):
                cols = slice(h * HD, (h + 1) * HD)
                vcols = slice(2 * D + h * HD, 2 * D + (h + 1) * HD)
                heads.append({"q": [(z[:, :, cols], NT)], "k": [(z[:, :, D + h * HD:D + (h + 1) * HD], NT), (kc[:, :, cols], 2)]})
                for t in range(NT):
                    it = {"values": [z[:, 0, vcols]], "out": z[:, t, cols], "head": h, "bias": None}
                    if t:
                        first = 6 - 2 * (t - 1)
                        it.update(values=[z[:, u, vcols] for u in range(1, NT)] + [vc[:, u, cols] for u in range(2)],
                                  bias=bias[:, h % NB, first:first + 8, :].rearrange("p r c -> p (r c)"))
                    items.append(it)
            at = Attention(K, att, heads, items, biased=True, bias_ready=s_masked, flip=flip)

            def load_bias(sp):
                sp.dma_start(outside[:], I["const_outside"]).then_inc(loaded.sem, 16)
                for h in range(C_HEADS):
                    if h >= NB:
                        sp.wait_ge(at.biasd.sem, at.biasd.at(2 * NT * (h - NB + 1)))
                    for r in range(2):
                        src = bass.AP(tensor=K.rpb_rows.tensor, offset=K.rpb_rows.offset + (h * 15 + 1 - r) * P,
                                      ap=[[1, HD], [P, DR], [1, HD]])
                        sp.dma_start(bias[r * HD:(r + 1) * HD, h % NB], src).then_inc(landed[h % NB].sem, 16)

            def mask_bias(pool, h):
                if h == 0:
                    pool.wait_ge(loaded.sem, loaded.at(16))
                pool.wait_ge(landed[h % NB].sem, landed[h % NB].at(32 * (h // NB + 1)))
                b = bias[:, h % NB]
                out = outside[:].rearrange("p (o c) -> p o c", o=1).broadcast_to([P, DR, HD])
                pool.tensor_tensor(b, b, out, ALU.add).then_inc(s_masked.sem, 1)
            attention_block(K, at, load_bias, mask_bias)
            loaded.base += 16
            s_masked.base += C_HEADS
            for s in landed:
                s.base += 32 * (C_HEADS // NB)



def rwkv_stage(K, zs):
    nc, I, O = K.nc, K.I, K.O
    CT = B_HEADS * HD // P
    ORDER = ((1, 2, 3, 4, 0), (4, 3, 2, 1, 0))
    LEVELS = 6
    NS = NT
    PIECES = ((0, 512), (512, T))
    R0, K0, V0, WD, AD, GD = 0, 4, 8, 12, 13, 14
    with ExitStack() as ctx:
        V = K.sb(ctx, "v_rows", [P, NT, CT * P])
        Y = K.sb(ctx, "y_chan", [P, CT, T])
        mask = K.sb(ctx, "masks", [P, 2, 2 * P])
        ST = K.sb(ctx, "state", [P, 2, CT, HD])
        SZ = K.sb(ctx, "state_zero", [P, HD])
        w2 = K.sb(ctx, "w2", [P, 2, CT * P])
        vec = K.sb(ctx, "channel_vectors", [P, 12, CT])
        KKG, KA, RK, LG, LB, W0, A0, OMKA, KEPS, GEPS = 0, 1, 2, 3, 4, 5, 7, 9, 10, 11
        ones2 = K.sb(ctx, "head_ones", [P, P])
        loaded = K.sig("loaded")
        s_turned, s_copied, s_spill = K.sig("qk_turned"), K.sig("qk_copied"), K.sig("x_moved")

        with ExitStack() as first:
            sin = K.sb(first, "state_in", [HD, 2, B_HEADS, HD])
            bank = K.ps(first, "rwkv_bank", [P, 2, 512])
            with nc.Block() as block:
                @block.sync
                def _(sp):
                    sp.dma_start(K.x_rows, K.x[:]).then_inc(s_spill.sem, 16)
                    for d, s in enumerate(("state_b_fwd", "state_b_bwd")):
                        sp.dma_start(sin[:, d], I[s][0, 0].rearrange("h i j -> i h j")).then_inc(loaded.sem, 16)
                    for n, (w, d) in enumerate((("b_w2", 0), ("b_w2", 1), ("b_a2", 0), ("b_a2", 1))):
                        sp.dma_start(w2[HD * d:HD * d + HD, n // 2], I[w][0, d]).then_inc(loaded.sem, 16)
                    sp.dma_start(mask[:], I["const_masks"]).then_inc(loaded.sem, 16)
                    sp.dma_start(ones2[:], I["const_head_ones"]).then_inc(loaded.sem, 16)
                    with nc.allow_non_contiguous_dma("vectors of 512 channels"):
                        for n, src in ((KKG, I["b_kk"][0]), (KA, I["b_ka"][0]), (RK, I["b_rk"][0].rearrange("h d -> (h d)")),
                                       (LG, I["b_ln_g"][0]), (LB, I["b_ln_b"][0]), (W0, I["b_w0"][0, 0]), (W0 + 1, I["b_w0"][0, 1]),
                                       (A0, I["b_a0"][0, 0]), (A0 + 1, I["b_a0"][0, 1])):
                            sp.dma_start(vec[:, n, :], src.rearrange("(c p) -> p c", p=P)).then_inc(loaded.sem, 16)

                @block.tensor
                def _(pe):
                    for t in range(NT):
                        if t >= 2:
                            pe.wait_ge(s_copied.sem, s_copied.at(t - 1))
                        for c in range(CT):
                            mm = pe.transpose(bank[:, t % 2, c * P:(c + 1) * P], zs[:, V0 + c, t * P:(t + 1) * P], K.ident[:])
                        mm.then_inc(s_turned.sem, 1)
                    pe.wait_ge(loaded.sem, loaded.at(16 * 17))
                    for d in range(2):
                        n = NT + d
                        pe.wait_ge(s_copied.sem, s_copied.at(n - 1))
                        for c in range(CT):
                            mm = pe.transpose(bank[:, n % 2, c * HD:(c + 1) * HD],
                                              sin[:, d, 2 * c:2 * c + 2, :].rearrange("i h j -> i (h j)"), K.ident[0:HD, 0:HD])
                        mm.then_inc(s_turned.sem, 1)

                @block.scalar
                def _(a):
                    a.activation(zs[:, WD, :], zs[:, WD, :], ACT.Tanh)
                    for t in range(NT):
                        a.wait_ge(s_turned.sem, s_turned.at(t + 1))
                        a.activation(V[:, t, :], bank[:, t % 2, :], ACT.Copy).then_inc(s_copied.sem, 1)
                    for d in range(2):
                        n = NT + d
                        a.wait_ge(s_turned.sem, s_turned.at(n + 1))
                        a.activation(ST[:, d], bank[:, n % 2, 0:CT * HD].rearrange("p (c i) -> p c i", c=CT), ACT.Copy).then_inc(s_copied.sem, 1)

                @block.vector
                def _(dve):
                    dve.wait_ge(loaded.sem, loaded.at(16 * 17))
                    dve.tensor_scalar(vec[:, OMKA, :], vec[:, KA, :], -1.0, 1.0, ALU.mult, ALU.add)

                @block.gpsimd
                def _(pool):
                    pool.memset(SZ[:], 0.0)
                    pool.memset(vec[:, KEPS, :], 1e-12)
                    pool.memset(vec[:, GEPS, :], GN_EPS)
            loaded.base += 16 * 17
            s_turned.base += NT + 2
            s_copied.base += NT + 2

        with ExitStack() as scan:
            xf = K.x[:].rearrange("p t d -> p (t d)")
            ZR = [[K.sb(scan, f"zr{d}", [P, NT, 2, P]) for d in range(2)],
                  [xf[:, 2 * T * d:2 * T * (d + 1)].rearrange("p (c a n) -> p c a n", c=NT, a=2) for d in range(2)]]
            Kt = [[K.sb(scan, f"kt{d}", [P, T])[:] for d in range(2)], [xf[:, (4 + d) * T:(5 + d) * T] for d in range(2)]]
            Bt = [[K.sb(scan, f"bt{d}", [P, T])[:] for d in range(2)], [xf[:, (6 + d) * T:(7 + d) * T] for d in range(2)]]
            em = [[K.sb(scan, f"em{par}{d}", [P, NT]) for d in range(2)] for par in range(2)]
            half_end = K.sb(scan, "half_end", [P, NT])
            kk, rs = K.sb(scan, "kk", [P, T]), K.sb(scan, "kk_rs", [P, T])
            lw, al, L, Lm, Lx, kd = (K.sb(scan, n, [P, T]) for n in ("log_decay", "iclr", "L", "L_centred", "L_before", "kd"))
            AM = K.sb(scan, "a_masked", [P, 2, 2, 2, 512])
            X = K.sb(scan, "a_power", [P, 2, 2, 2, 2, P])
            W = K.sb(scan, "inverse_so_far", [P, 2, 2, 2, P])
            TF = K.sb(scan, "inverse_t", [P, 2, 2, 2, P])
            KB = K.sb(scan, "kb_rows", [P, 2, 2, 2 * P])
            Sm = K.sb(scan, "state_mid", [P, 2, P])
            Rb, Ub = K.sb(scan, "rhs", [P, 2, P]), K.sb(scan, "u", [P, 2, P])
            tmp = K.sb(scan, "state_sum", [P, 2, HD])
            pU = [K.ps(scan, f"p_unit{d}", [P, 3, 512]) for d in range(2)]
            pC = K.ps(scan, "p_chain", [P, 2, 512])
            names = ("raw", "sq", "prod", "eps", "rs", "kk", "sig", "lw", "scan", "half", "lm", "lx", "exp", "kd", "tilde")
            (s_raw, s_sq, s_prod, s_eps, s_rs, s_kk, s_sig, s_lw, s_scan, s_half, s_lm, s_lx, s_exp, s_kd, s_tilde) = (
                K.sig("rw_" + n) for n in names)
            u_rest = K.sig("un_rest")
            names = ("xk", "a", "am", "xt", "x0", "kb", "tt0")
            (u_xk, u_m, u_am, u_xt, u_x0, u_kb, u_tt0) = (K.sig("un_" + n) for n in names)
            u_sq, u_xw, u_iv, u_tt = ([K.sig(f"un_{n}{d}") for d in range(2)] for n in ("squared", "power", "times", "inverse"))
            names = ("s", "r", "rb", "u", "ub", "end", "y", "sum", "state", "out")
            (c_s, c_r, c_rb, c_u, c_ub, c_end, c_y, c_sum, c_st, c_out) = (K.sig("ch_" + n) for n in names)

            def cols(ap, c):
                return ap[:, c * P:(c + 1) * P]

            def z_r(ct, d, c):
                return ZR[ct % 2][d][:, c]

            def chunks(ap):
                return ap[:].rearrange("p (c n) -> p c n", c=NT)

            def cols_of(ct):
                return slice(ct * P, (ct + 1) * P)

            def pair_pe(pe, ct, k, lhs, rhs):
                if k == 1:
                    pe.wait_ge(s_eps.sem, s_eps.at(2 * ct + 2))
                elif ct or k:
                    pe.wait_ge(s_sig.sem, s_sig.at(8 * ct + 2 * max(k - 1, 0)))
                if ct:
                    q = 2 * (NS * (ct - 1) + PAIR_STEP[k]) + 1
                    pe.wait_ge(u_x0.sem, u_x0.at(q + 1))
                for i, (a, b) in enumerate(PIECES):
                    pe.matmul(pU[i][:, 2, 0:b - a], lhs, rhs[:, a:b], start=True, stop=True).then_inc(s_prod.sem, 1)

            def squares_act(a, ct):
                if ct:
                    a.wait_ge(s_tilde.sem, s_tilde.at(8 * ct))
                a.activation(kk[:], zs[:, K0 + ct, :], ACT.Copy, scale=vec[:, KKG, ct:ct + 1]).then_inc(s_raw.sem, 1)
                a.activation(rs[:], zs[:, K0 + ct, :], ACT.Square, scale=vec[:, KKG, ct:ct + 1]).then_inc(s_sq.sem, 1)

            def norm_pe(pe, ct):
                pe.wait_ge(s_sq.sem, s_sq.at(ct + 1))
                pair_pe(pe, ct, 0, ones2[:], rs)

            def norm_act(a, ct):
                for i, (x, y) in enumerate(PIECES):
                    a.wait_ge(s_prod.sem, s_prod.at(10 * ct + i + 1))
                    a.activation(lw[:, x:y], pU[i][:, 2, 0:y - x], ACT.Sqrt, bias=vec[:, KEPS, 0:1]).then_inc(s_eps.sem, 1)

            def norm_dve(dve, ct):
                dve.wait_ge(s_eps.sem, s_eps.at(2 * ct + 2))
                dve.reciprocal(rs[:], lw[:]).then_inc(s_rs.sem, 1)
                dve.wait_ge(s_rs.sem, s_rs.at(ct + 1))
                dve.wait_ge(s_raw.sem, s_raw.at(ct + 1))
                dve.tensor_tensor(kk[:], kk[:], rs[:], ALU.mult).then_inc(s_kk.sem, 1)

            def lora_pe(d, w):
                rows = slice(HD * d, HD * d + HD)
                return lambda pe, ct: pair_pe(pe, ct, 1 + 2 * d + w, w2[rows, w, cols_of(ct)], zs[rows, WD + w, :])

            def lora_act(d, w):
                def f(a, ct):
                    if w == 0:
                        if d:
                            a.wait_ge(s_tilde.sem, s_tilde.at(8 * ct + 4))
                        else:
                            a.wait_ge(s_rs.sem, s_rs.at(ct + 1))
                    out, bias = ((lw, W0), (al, A0))[w]
                    for i, (x, y) in enumerate(PIECES):
                        a.wait_ge(s_prod.sem, s_prod.at(10 * ct + 2 + 4 * d + 2 * w + i + 1))
                        a.activation(out[:, x:y], pU[i][:, 2, 0:y - x], ACT.Sigmoid, bias=vec[:, bias + d, ct:ct + 1]).then_inc(s_sig.sem, 1)
                return f

            def decay_pool(d):
                def f(pool, ct):
                    pool.wait_ge(s_sig.sem, s_sig.at(8 * ct + 4 * d + 2))
                    pool.tensor_scalar(lw[:], lw[:], -DECAY, None, ALU.mult).then_inc(s_lw.sem, 1)
                return f

            def scan_dve(d):
                def f(dve, ct):
                    n = 2 * ct + d
                    dve.wait_ge(s_lw.sem, s_lw.at(n + 1))
                    for c in range(NT):
                        dve.tensor_tensor_scan(cols(L, c), K.ones[:].broadcast_to([P, P]), cols(lw, c), 0.0, ALU.mult, ALU.add).then_inc(s_scan.sem, 1)
                    dve.wait_ge(s_scan.sem, s_scan.at(NT * (n + 1)))
                    dve.tensor_scalar(half_end[:], chunks(L)[:, :, P - 1], 0.5, None, ALU.mult).then_inc(s_half.sem, 1)
                return f

            def rate_pool(d):
                def f(pool, ct):
                    n = 2 * ct + d
                    pool.wait_ge(s_sig.sem, s_sig.at(8 * ct + 4 * d + 4))
                    pool.tensor_scalar(kd[:], al[:], vec[:, KA, ct:ct + 1], vec[:, OMKA, ct:ct + 1], ALU.mult, ALU.add).then_inc(s_kd.sem, 1)
                    pool.wait_ge(s_kd.sem, s_kd.at(3 * n + 1))
                    pool.tensor_tensor(kd[:], kd[:], zs[:, K0 + ct, :], ALU.mult).then_inc(s_kd.sem, 1)
                    pool.wait_ge(s_kk.sem, s_kk.at(ct + 1))
                    pool.tensor_tensor(al[:], al[:], kk[:], ALU.mult).then_inc(s_kd.sem, 1)
                return f

            def centre_dve(d):
                def f(dve, ct):
                    dve.wait_ge(s_half.sem, s_half.at(2 * ct + d + 1))
                    h = half_end[:].rearrange("p (c o) -> p c o", o=1).broadcast_to([P, NT, P])
                    if d == 0:
                        dve.tensor_tensor(chunks(Lm), chunks(L), h, ALU.subtract).then_inc(s_lm.sem, 1)
                    else:
                        dve.tensor_tensor(chunks(Lx), h, chunks(L), ALU.subtract).then_inc(s_lx.sem, 1)
                return f

            def other_pool(d):
                def f(pool, ct):
                    n = 2 * ct + d
                    if d == 0:
                        pool.wait_ge(s_lm.sem, s_lm.at(n + 1))
                        pool.tensor_tensor(Lx[:], Lm[:], lw[:], ALU.subtract).then_inc(s_lx.sem, 1)
                    else:
                        pool.wait_ge(s_lx.sem, s_lx.at(n + 1))
                        pool.tensor_tensor(Lm[:], Lx[:], lw[:], ALU.add).then_inc(s_lm.sem, 1)
                return f

            def middle_act(d):
                def f(a, ct):
                    a.wait_ge(s_half.sem, s_half.at(2 * ct + d + 1))
                    if ct >= 2:
                        a.wait_ge(c_st.sem, c_st.at(2 * NS * (ct - 1)))
                    a.activation(em[ct % 2][d][:], half_end[:], ACT.Exp).then_inc(s_exp.sem, 1)
                return f

            def exps_act(d):
                def f(a, ct):
                    n = 2 * ct + d
                    a.wait_ge(s_lm.sem, s_lm.at(n + 1))
                    a.wait_ge(s_lx.sem, s_lx.at(n + 1))
                    a.activation(L[:], Lm[:], ACT.Exp, scale=-1.0).then_inc(s_exp.sem, 1)
                    a.wait_ge(s_exp.sem, s_exp.at(4 * n + 2))
                    a.activation(Lm[:], Lm[:], ACT.Exp).then_inc(s_exp.sem, 1)
                    a.activation(Lx[:], Lx[:], ACT.Exp).then_inc(s_exp.sem, 1)
                return f

            def tilde_dve(d):
                def f(dve, ct):
                    n, par = 2 * ct + d, ct % 2
                    dve.wait_ge(s_exp.sem, s_exp.at(4 * n + 4))
                    dve.wait_ge(s_kd.sem, s_kd.at(3 * n + 3))
                    dve.wait_ge(s_kk.sem, s_kk.at(ct + 1))
                    if ct >= 2:
                        dve.wait_ge(c_y.sem, c_y.at(2 * NS * (ct - 1)))
                    elif ct == 1 and d == 0:
                        dve.wait_ge(s_spill.sem, s_spill.at(16))
                    dve.tensor_tensor(ZR[par][d][:, :, 1, :], chunks_of(zs[:, R0 + ct, :]), chunks(Lm), ALU.mult).then_inc(s_tilde.sem, 1)
                    dve.scalar_tensor_tensor(ZR[par][d][:, :, 0, :], chunks(kk), -1.0, chunks(Lx), ALU.mult, ALU.mult).then_inc(s_tilde.sem, 1)
                    dve.tensor_tensor(Kt[par][d], kd[:], L[:], ALU.mult).then_inc(s_tilde.sem, 1)
                    dve.tensor_tensor(Bt[par][d], al[:], L[:], ALU.mult).then_inc(s_tilde.sem, 1)
                return f

            PREP = [((0, 1), "act", squares_act), ((0, 3), "pe", norm_pe), ((0, 3), "act", norm_act), ((0, 5), "dve", norm_dve)]
            for d, i in ((0, 1), (1, 3)):
                PREP += [((i, 1), "pe", lora_pe(d, 0)), ((i, 1), "act", lora_act(d, 0)), ((i, 2), "pool", decay_pool(d)),
                         ((i, 3), "pe", lora_pe(d, 1)), ((i, 3), "act", lora_act(d, 1)), ((i, 4), "dve", scan_dve(d)),
                         ((i, 5), "pool", rate_pool(d)), ((i, 5), "dve", centre_dve(d)), ((i, 6), "pool", other_pool(d)),
                         ((i, 6), "act", middle_act(d)), ((i + 1, 2), "act", exps_act(d)), ((i + 1, 5), "dve", tilde_dve(d))]
            PAIR_STEP = (0, 1, 1, 3, 3)

            def chunks_of(ap):
                return ap.rearrange("p (c n) -> p c n", c=NT)

            def unit(ct, i, d):
                s = NS * ct + i
                return 2 * s + d, s, ORDER[d][i], s % 2

            def head(hh):
                return slice(HD * hh, HD * hh + HD)

            def products_pe(pe, ct, i, d):
                q, s, c, par = unit(ct, i, d)
                pe.wait_ge(s_tilde.sem, s_tilde.at(8 * ct + 4 * d + 4))
                if s:
                    pe.wait_ge(u_tt[d].sem, u_tt[d].at(LEVELS * s))
                pX, pM = pU[d][:, 2, :], pU[d][:, 0:2, :]
                pairs = [k for k in range(5) if PAIR_STEP[k] < i] if ct + 1 < CT else []
                last, k = (ct + 1, pairs[-1]) if pairs else (ct, 4)
                if k == 0:
                    pe.wait_ge(s_eps.sem, s_eps.at(2 * last + 2))
                else:
                    pe.wait_ge(s_sig.sem, s_sig.at(8 * last + 2 * k))
                pe.transpose(pX[:, 2 * P:3 * P], cols(Kt[ct % 2][d], c), K.ident[:])
                pe.transpose(pX[:, 3 * P:4 * P], cols(Bt[ct % 2][d], c), K.ident[:]).then_inc(u_xk.sem, 1)
                for n, op in enumerate((Bt, Kt)):
                    for hh in range(2):
                        zr = z_r(ct, d, c)[head(hh)].rearrange("p a n -> p (a n)")
                        mm = pe.matmul(pM[:, hh, 2 * n * P:2 * (n + 1) * P], op[ct % 2][d][head(hh), c * P:(c + 1) * P], zr, start=True, stop=True)
                mm.then_inc(u_m.sem, 1)

            def turn_pe(pe, ct, i, d):
                q, s, c, par = unit(ct, i, d)
                pe.wait_ge(u_am.sem, u_am.at(q + 1))
                pe.wait_ge(u_kb.sem, u_kb.at(q + 1))
                for hh in range(2):
                    mm = pe.transpose(pU[d][:, 2, hh * P:(hh + 1) * P], AM[:, par, d, hh, 0:P], K.ident[:])
                mm.then_inc(u_xt.sem, 1)

            def level_pe(pe, ct, i, d, l):
                q, s, c, par = unit(ct, i, d)
                pA, pI = pU[d][:, 0, :], pU[d][:, 1, :]
                if l == 0:
                    pe.wait_ge(u_x0.sem, u_x0.at(q + 1))
                    pe.wait_ge(u_rest.sem, u_rest.at(2 * q + 2))
                else:
                    pe.wait_ge(u_xw[d].sem, u_xw[d].at(LEVELS * s + l))
                cur = l % 2
                if l < LEVELS:
                    for hh in range(2):
                        x = X[:, cur, d, hh, 1, :]
                        xt = AM[:, par, d, hh, 0:P] if l == 0 else X[:, cur, d, hh, 0, :]
                        if l < LEVELS - 1:
                            pe.matmul(pA[:, 2 * hh * P:(2 * hh + 1) * P], x, xt, start=True, stop=True)
                        mm = pe.matmul(pA[:, (2 * hh + 1) * P:(2 * hh + 2) * P], xt, x, start=True, stop=True)
                    mm.then_inc(u_sq[d].sem, 1)
                if l:
                    if l == 1:
                        pe.wait_ge(u_tt0.sem, u_tt0.at(q + 1))
                    else:
                        pe.wait_ge(u_tt[d].sem, u_tt[d].at(LEVELS * s + l - 1))
                    for hh in range(2):
                        mm = pe.matmul(pI[:, hh * P:(hh + 1) * P], X[:, cur, d, hh, 1, :], W[:, cur, d, hh, :], start=True, stop=True)
                    mm.then_inc(u_iv[d].sem, 1)

            def chain_r(pe, ct, i, d):
                q, s, c, par = unit(ct, i, d)
                pe.wait_ge(c_s.sem, c_s.at(q + 1))
                if q >= 2:
                    pe.wait_ge(c_out.sem, c_out.at(q - 1))
                for hh in range(2):
                    pe.matmul(pC[:, d, hh * HD:(hh + 1) * HD], AM[:, par, d, hh, 2 * P:3 * P], V[:, c, ct * P + hh * HD:ct * P + (hh + 1) * HD],
                              start=hh == 0, stop=False)
                mm = pe.matmul(pC[:, d, 0:P], z_r(ct, d, c)[:, 0, :], Sm[:, d, :], start=False, stop=True)
                mm.then_inc(c_r.sem, 1)

            def chain_u(pe, ct, i, d):
                q, s, c, par = unit(ct, i, d)
                pe.wait_ge(c_rb.sem, c_rb.at(q + 1))
                pe.wait_ge(u_tt[d].sem, u_tt[d].at(LEVELS * (s + 1)))
                for hh in range(2):
                    mm = pe.matmul(pC[:, d, hh * HD:(hh + 1) * HD], TF[:, par, d, hh, :], Rb[:, d, hh * HD:(hh + 1) * HD], start=True, stop=True)
                mm.then_inc(c_u.sem, 1)

            def chain_end(pe, ct, i, d):
                q, s, c, par = unit(ct, i, d)
                pe.wait_ge(c_ub.sem, c_ub.at(q + 1))
                pe.wait_ge(u_kb.sem, u_kb.at(q + 1))
                for hh in range(2):
                    out = pC[head(hh), d, P:P + HD]
                    v = V[:, c, ct * P + hh * HD:ct * P + (hh + 1) * HD]
                    pe.matmul(out, KB[:, par, d, P + hh * HD:P + (hh + 1) * HD], Ub[:, d, hh * HD:(hh + 1) * HD], start=True, stop=False)
                    mm = pe.matmul(out, KB[:, par, d, hh * HD:(hh + 1) * HD], v, start=False, stop=True)
                mm.then_inc(c_end.sem, 1)
                for hh in range(2):
                    out = pC[head(hh), d, 0:P]
                    v = V[:, c, ct * P + hh * HD:ct * P + (hh + 1) * HD]
                    pe.matmul(out, Ub[:, d, hh * HD:(hh + 1) * HD], AM[:, par, d, hh, P:2 * P], start=True, stop=False)
                    pe.matmul(out, v, AM[:, par, d, hh, 3 * P:4 * P], start=False, stop=False)
                mm = pe.matmul(pC[:, d, 0:P], Sm[:, d, :], z_r(ct, d, c)[:, 1, :], start=False, stop=True)
                mm.then_inc(c_y.sem, 1)

            def kb_act(a, ct, i, d):
                q, s, c, par = unit(ct, i, d)
                a.wait_ge(u_xk.sem, u_xk.at(q + 1))
                if q >= 4:
                    a.wait_ge(c_y.sem, c_y.at(q - 3))
                a.activation(KB[:, par, d, :], pU[d][:, 2, 2 * P:4 * P], ACT.Copy).then_inc(u_kb.sem, 1)

            def power_act(a, ct, i, d):
                q, s, c, par = unit(ct, i, d)
                a.wait_ge(u_xt.sem, u_xt.at(q + 1))
                if s:
                    a.wait_ge(u_iv[d].sem, u_iv[d].at(LEVELS * s))
                a.activation(X[:, 0, d, :, 1, :], pU[d][:, 2, 0:2 * P].rearrange("p (h n) -> p h n", h=2), ACT.Copy).then_inc(u_x0.sem, 1)

            def level_act(a, ct, i, d, l):
                q, s, c, par = unit(ct, i, d)
                a.wait_ge(u_sq[d].sem, u_sq[d].at(LEVELS * s + l + 1))
                if l:
                    a.wait_ge(u_iv[d].sem, u_iv[d].at(LEVELS * s + l - 1))
                if l < LEVELS - 1:
                    out, src = X[:, (l + 1) % 2, d].rearrange("p h x n -> p (h x n)"), pU[d][:, 0, :]
                else:
                    out, src = X[:, (l + 1) % 2, d, :, 1, :], pU[d][:, 0, :].rearrange("p (h x n) -> p h x n", h=2, x=2)[:, :, 1, :]
                a.activation(out, src, ACT.Copy).then_inc(u_xw[d].sem, 1)

            def ub_act(a, ct, i, d):
                q, s, c, par = unit(ct, i, d)
                a.wait_ge(c_u.sem, c_u.at(q + 1))
                if q >= 2:
                    a.wait_ge(c_y.sem, c_y.at(q - 1))
                a.activation(Ub[:, d, :], pC[:, d, 0:P], ACT.Copy).then_inc(c_ub.sem, 1)

            def masks_dve(dve, ct, i, d):
                q, s, c, par = unit(ct, i, d)
                dve.wait_ge(u_m.sem, u_m.at(q + 1))
                if q >= 4:
                    dve.wait_ge(c_y.sem, c_y.at(q - 3))
                dve.tensor_tensor(AM[:, par, d, :, 0:P], pU[d][:, 0:2, 0:P], mask[:, d:d + 1, 0:P].broadcast_to([P, 2, P]), ALU.mult).then_inc(u_am.sem, 1)

            def masks_rest_dve(dve, ct, i, d):
                q, s, c, par = unit(ct, i, d)
                dve.tensor_tensor(AM[:, par, d, :, P:2 * P], pU[d][:, 0:2, P:2 * P], mask[:, d:d + 1, P:2 * P].broadcast_to([P, 2, P]),
                                  ALU.mult).then_inc(u_rest.sem, 1)
                dve.tensor_tensor(AM[:, par, d, :, 2 * P:4 * P], pU[d][:, 0:2, 2 * P:4 * P], mask[:, d:d + 1, :].broadcast_to([P, 2, 2 * P]),
                                  ALU.mult).then_inc(u_rest.sem, 1)

            def inverse_dve(dve, ct, i, d, l):
                q, s, c, par = unit(ct, i, d)
                dve.wait_ge(u_iv[d].sem, u_iv[d].at(LEVELS * s + l))
                if l == 1:
                    dve.wait_ge(u_tt0.sem, u_tt0.at(q + 1))
                else:
                    dve.wait_ge(u_tt[d].sem, u_tt[d].at(LEVELS * s + l - 1))
                out = W[:, (l + 1) % 2, d] if l < LEVELS else TF[:, par, d]
                if l == LEVELS and q >= 4:
                    dve.wait_ge(c_y.sem, c_y.at(q - 3))
                dve.tensor_tensor(out, W[:, l % 2, d], pU[d][:, 1, 0:2 * P].rearrange("p (h n) -> p h n", h=2), ALU.add).then_inc(u_tt[d].sem, 1)

            def state_dve(dve, ct, i, d):
                q, s, c, par = unit(ct, i, d)
                dve.wait_ge(s_exp.sem, s_exp.at(8 * ct + 4 * d + 1))
                if q >= 2:
                    dve.wait_ge(c_st.sem, c_st.at(q - 1))
                    dve.wait_ge(c_y.sem, c_y.at(q - 1))
                start = ST[:, d, ct, :] if i < NS - 1 else SZ[:]
                start = start.rearrange("p (o i) -> p o i", o=1).broadcast_to([P, 2, HD])
                dve.scalar_tensor_tensor(Sm[:, d, :].rearrange("p (h i) -> p h i", h=2), start, em[ct % 2][d][:, c:c + 1],
                                         ones2[:].rearrange("p (h i) -> p h i", h=2), ALU.mult, ALU.mult).then_inc(c_s.sem, 1)

            def rb_dve(dve, ct, i, d):
                q, s, c, par = unit(ct, i, d)
                dve.wait_ge(c_r.sem, c_r.at(q + 1))
                dve.tensor_copy(Rb[:, d, :], pC[:, d, 0:P]).then_inc(c_rb.sem, 1)

            def end_dve(dve, ct, i, d):
                q, s, c, par = unit(ct, i, d)
                dve.wait_ge(c_y.sem, c_y.at(q + 1))
                start = ST[:, d, ct, :] if i < NS - 1 else SZ[:]
                dve.scalar_tensor_tensor(tmp[:, d, :], start, em[ct % 2][d][:, c:c + 1], pC[:, d, P:P + HD], ALU.mult, ALU.add).then_inc(c_sum.sem, 1)
                dve.wait_ge(c_sum.sem, c_sum.at(q + 1))
                dve.tensor_scalar(ST[:, d, ct, :], tmp[:, d, :], em[ct % 2][d][:, c:c + 1], None, ALU.mult).then_inc(c_st.sem, 1)
                y, p = Y[:, ct, c * P:(c + 1) * P], pC[:, d, 0:P]
                other = 2 * (NS * ct + ORDER[1 - d].index(c)) + 1 - d
                if other > q:
                    dve.tensor_copy(y, p).then_inc(c_out.sem, 1)
                else:
                    dve.wait_ge(c_out.sem, c_out.at(other + 1))
                    dve.tensor_tensor(y, p, y, ALU.add).then_inc(c_out.sem, 1)

            steps = [(ct, i) for ct in range(CT) for i in range(NS)]

            def walk(eng, name, starts, level, chain):
                def prepare(ct, slot=None):
                    for at, who, piece in PREP:
                        if who == name and slot in (None, at):
                            piece(eng, ct)
                prepare(0)
                for n in range(len(steps) + 1):
                    for start in starts:
                        for d in range(2):
                            if n < len(steps):
                                start(eng, *steps[n], d)
                    for l in range(LEVELS + 1):
                        for d in range(2):
                            if n < len(steps):
                                level(eng, *steps[n], d, l)
                        for link in chain.get(l, ()):
                            for d in range(2):
                                if n:
                                    link(eng, *steps[n - 1], d)
                        if n < len(steps) and steps[n][0] + 1 < CT:
                            prepare(steps[n][0] + 1, (steps[n][1], l))

            with nc.Block() as block:
                @block.tensor
                def _(pe):
                    walk(pe, "pe", (products_pe, turn_pe), level_pe, {0: (chain_r,), 2: (chain_u,), 4: (chain_end,)})

                @block.scalar
                def _(a):
                    def level(a, ct, i, d, l):
                        if l < LEVELS:
                            level_act(a, ct, i, d, l)
                    walk(a, "act", (kb_act, power_act), level, {2: (ub_act,)})

                @block.vector
                def _(dve):
                    def level(dve, ct, i, d, l):
                        if l:
                            inverse_dve(dve, ct, i, d, l)
                    walk(dve, "dve", (masks_dve, masks_rest_dve), level, {0: (state_dve, rb_dve), 4: (end_dve,)})

                @block.gpsimd
                def _(pool):
                    def first_power(pool, ct, i, d):
                        q, s, c, par = unit(ct, i, d)
                        pool.wait_ge(u_am.sem, u_am.at(q + 1))
                        if s:
                            pool.wait_ge(u_tt[d].sem, u_tt[d].at(LEVELS * s))
                        eye = K.ident[:].rearrange("p (o n) -> p o n", o=1).broadcast_to([P, 2, P])
                        pool.tensor_tensor(W[:, 1, d], AM[:, par, d, :, 0:P], eye, ALU.add).then_inc(u_tt0.sem, 1)
                    walk(pool, "pool", (first_power,), lambda *x: None, {})
            for s, n in ((s_raw, 1), (s_sq, 1), (s_prod, 10), (s_eps, 2), (s_rs, 1), (s_kk, 1), (s_sig, 8), (s_lw, 2), (s_scan, 2 * NT),
                         (s_half, 2), (s_lm, 2), (s_lx, 2), (s_exp, 8), (s_kd, 6), (s_tilde, 8)):
                s.base += n * CT
            u_rest.base += 4 * len(steps)
            for s in (u_xk, u_m, u_am, u_xt, u_x0, u_kb, u_tt0, c_s, c_r, c_rb, c_u, c_ub, c_end, c_y, c_sum, c_st, c_out):
                s.base += 2 * len(steps)
            for d in range(2):
                for sig in (u_sq[d], u_xw[d], u_iv[d], u_tt[d]):
                    sig.base += LEVELS * len(steps)

        with ExitStack() as last:
            a1, a2, a3 = (K.sb(last, n, [P, T]) for n in ("gn_a", "gn_b", "gn_c"))
            g2 = K.sb(last, "g2", [P, CT * P])
            so = K.sb(last, "state_out", [HD, 2, B_HEADS, HD])
            pN = K.ps(last, "p_sums", [P, 1024])
            pQ = K.ps(last, "p_squares", [P, 1024])
            pG = K.ps(last, "p_gate", [P, 1024])
            pS = K.ps(last, "p_states", [P, 512])
            names = ("rk", "sumpe", "mean", "sq", "varpe", "var", "rstd", "gate", "hi")
            g_sig = {n: K.sig("gn_" + n) for n in names}
            g_v = K.sig("gn_steps")
            s_out, loaded3 = K.sig("qk_stored"), K.sig("loaded")
            s_st, s_so = K.sig("qk_turned"), K.sig("qk_copied")
            NV = 8
            bonus = pQ

            def sums(pe, out, src):
                for a, b in PIECES:
                    mm = pe.matmul(out[:, a:b], ones2[:], src[:, a:b], start=True, stop=True)
                return mm

            with nc.Block() as block:
                @block.sync
                def _(sp):
                    sp.dma_start(g2[:], I["b_g2"][0]).then_inc(loaded3.sem, 16)
                    sp.dma_start(K.x[:], K.x_rows).then_inc(s_spill.sem, 16)
                    sp.wait_ge(s_spill.sem, s_spill.at(32))
                    sp.wait_ge(s_so.sem, s_so.at(2))
                    for d, o in enumerate(("new_state_b_fwd", "new_state_b_bwd")):
                        sp.dma_start(O[o][0, 0].rearrange("h i j -> i h j"), so[:, d]).then_inc(s_out.sem, 16)
                    sp.wait_ge(s_out.sem, s_out.at(32))

                @block.scalar
                def _(a):
                    a.activation(zs[:, GD, :], zs[:, GD, :], ACT.Sigmoid).then_inc(g_sig["gate"].sem, 1)
                    for d in range(2):
                        a.wait_ge(s_st.sem, s_st.at(d + 1))
                        a.activation(so[:, d].rearrange("i h j -> i (h j)"), pS[0:HD, :], ACT.Copy).then_inc(s_so.sem, 1)
                    for ct in range(CT):
                        a.wait_ge(g_v.sem, g_v.at(NV * ct + 2))
                        a.activation(a1[:], Y[:, ct, :], ACT.Square).then_inc(g_sig["sq"].sem, 1)
                        a.wait_ge(g_sig["varpe"].sem, g_sig["varpe"].at(ct + 1))
                        a.activation(a3[:], pN[:, 0:T], ACT.Sqrt, bias=vec[:, GEPS, 0:1], scale=1.0 / HD).then_inc(g_sig["rstd"].sem, 1)
                        a.wait_ge(g_v.sem, g_v.at(NV * ct + NV - 1))
                        a.activation(K.h_hi[:, CT + ct, :], Y[:, ct, :], ACT.Copy).then_inc(g_sig["hi"].sem, 1)

                @block.tensor
                def _(pe):
                    for d in range(2):
                        if d:
                            pe.wait_ge(s_so.sem, s_so.at(1))
                        for ct in range(CT):
                            mm = pe.transpose(pS[0:HD, ct * P:(ct + 1) * P], ST[:, d, ct, :], K.ident[:])
                        mm.then_inc(s_st.sem, 1)
                    pe.wait_ge(g_sig["gate"].sem, g_sig["gate"].at(1))
                    pe.wait_ge(loaded3.sem, loaded3.at(16))
                    for ct in range(CT):
                        if ct:
                            pe.wait_ge(g_v.sem, g_v.at(NV * ct - 1))
                        sums(pe, pN, Y[:, ct, :]).then_inc(g_sig["sumpe"].sem, 1)
                        pe.wait_ge(g_v.sem, g_v.at(NV * ct + 1))
                        sums(pe, bonus, a2[:]).then_inc(g_sig["sumpe"].sem, 1)
                        for a, b in PIECES:
                            mm = pe.matmul(pG[:, a:b], g2[:, ct * P:(ct + 1) * P], zs[:, GD, a:b], start=True, stop=True)
                        mm.then_inc(g_sig["sumpe"].sem, 1)
                        pe.wait_ge(g_sig["sq"].sem, g_sig["sq"].at(ct + 1))
                        sums(pe, pN, a1[:]).then_inc(g_sig["varpe"].sem, 1)

                @block.vector
                def _(dve):
                    def step(ins, n):
                        ins.then_inc(g_v.sem, 1)
                        dve.wait_ge(g_v.sem, g_v.at(n))
                    for ct in range(CT):
                        y, n = Y[:, ct, :], NV * ct
                        step(dve.scalar_tensor_tensor(a2[:], zs[:, R0 + ct, :], vec[:, RK, ct:ct + 1], zs[:, K0 + ct, :], ALU.mult, ALU.mult), n + 1)
                        dve.wait_ge(g_sig["sumpe"].sem, g_sig["sumpe"].at(3 * ct + 1))
                        step(dve.scalar_tensor_tensor(y, pN[:, 0:T], -1.0 / HD, y, ALU.mult, ALU.add), n + 2)
                        dve.wait_ge(g_sig["sumpe"].sem, g_sig["sumpe"].at(3 * ct + 3))
                        step(dve.tensor_tensor(a2[:], zs[:, V0 + ct, :], bonus[:, 0:T], ALU.mult), n + 3)
                        dve.wait_ge(g_sig["rstd"].sem, g_sig["rstd"].at(ct + 1))
                        step(dve.reciprocal(a3[:], a3[:]), n + 4)
                        step(dve.scalar_tensor_tensor(y, y, vec[:, LG, ct:ct + 1], a3[:], ALU.mult, ALU.mult), n + 5)
                        step(dve.scalar_tensor_tensor(y, y, vec[:, LB, ct:ct + 1], a2[:], ALU.add, ALU.add), n + 6)
                        step(dve.tensor_tensor(y, y, pG[:, 0:T], ALU.mult), n + 7)
                        dve.wait_ge(g_sig["hi"].sem, g_sig["hi"].at(ct + 1))
                        step(dve.tensor_tensor(K.h_lo[:, CT + ct, :], y, K.h_hi[:, CT + ct, :], ALU.subtract), n + 8)
            loaded3.base += 16
            s_spill.base += 32
            s_out.base += 32
            s_st.base += 2
            s_so.base += 2
            g_v.base += NV * CT
            for n, k in (("sumpe", 3 * CT), ("sq", CT), ("varpe", CT), ("rstd", CT), ("gate", 1), ("hi", CT)):
                g_sig[n].base += k



def route_stage(K, expert_of):
    nc, I = K.nc, K.I
    E = N_EXP
    with ExitStack() as ctx:
        bank = K.ps(ctx, "norm_bank", [P, 2, 512])
        norm = Norm(K, ctx, 1, 1, bank, store=K.h_rows)
        lg = K.ps(ctx, "p_logits", [P, NT, E])
        rk = K.ps(ctx, "p_rank", [P, NT, E])
        ct_ = K.ps(ctx, "p_count", [P, E])
        rw = K.sb(ctx, "router_w", [P, J, E])
        rb = K.sb(ctx, "router_b", [P, E])
        h32 = K.sb(ctx, "h_turned", [P, J, P])
        mask, ones = K.sb(ctx, "earlier", [P, P]), K.sb(ctx, "all_ones", [P, P])
        small = K.sb(ctx, "iotas", [P, 40])
        logits, biased, m1, m2, ms, pos, tmp = (K.sb(ctx, n, [P, NT, E]) for n in
                                                ("logits", "logits_b", "choice0", "choice1", "chosen", "position", "picked"))
        mx, ix, ixf = K.sb(ctx, "top", [P, NT, E]), K.sb(ctx, "top_i", [P, NT, E], U32), K.sb(ctx, "top_f", [P, NT, 2])
        lv = K.sb(ctx, "choice_logits", [P, 6, NT])
        cnt, nt, incl = (K.sb(ctx, n, [P, E]) for n in ("count", "tiles", "tiles_end"))
        part = K.sb(ctx, "tiles_part", [P, 5, E])
        te, tef = K.sb(ctx, "tile_cmp", [P, SLOT_TILES, E]), K.sb(ctx, "tile_expert", [P, SLOT_TILES])
        tok = K.sb(ctx, "token_ids", [P, NT], I32)
        zero = K.sb(ctx, "slot_zero", [1, SLOTS], I32)
        loaded, s_log, s_rank, s_v, s_z, s_exp = K.sig("loaded"), K.sig("rt_logits"), K.sig("rt_rank"), K.sig("gn_steps"), K.sig("rt_zero"), K.sig("rt_exp")
        s_cleared, s_scatter, s_h = K.sig("rt_cleared"), K.sig("rt_scattered"), K.sig("rt_h")
        steps = [0]

        with nc.Block() as block:
            @block.sync
            def _(sp):
                norm.load(sp)
                sp.dma_start(rw[:], rows_by_partition(I["router_w"][0])).then_inc(loaded.sem, 16)
                sp.dma_start(rb[:], I["router_b"].broadcast_to([P, E])).then_inc(loaded.sem, 16)
                sp.dma_start(mask[:], I["const_masks"][:, 0, 0:P]).then_inc(loaded.sem, 16)
                sp.dma_start(small[:], I["const_iotas"]).then_inc(loaded.sem, 16)
                sp.dma_start(tok[:], I["const_tokens"]).then_inc(loaded.sem, 16)
                sp.wait_ge(s_z.sem, s_z.at(1))
                sp.dma_start(K.tokens_of_slots.rearrange("s o -> o s"), zero[:]).then_inc(s_cleared.sem, 16)
                norm.store_rows(sp)

            @block.scalar
            def _(a):
                norm.squares(a)
                for n in range(2 * NT):
                    a.wait_ge(norm.turned.sem, norm.turned.at(n + 1))
                    t, half = divmod(n, 2)
                    src = bank[:, n % 2, :].rearrange("p (j n) -> p j n", j=4)
                    if half == 0 and t:
                        a.wait_ge(s_log.sem, s_log.at(t))
                    a.activation(h32[:, 4 * half:4 * half + 4, :], src, ACT.Copy).then_inc(s_h.sem, 1)
                a.wait_ge(s_v.sem, s_v.at(V_EXP))
                a.activation(lv[:, 2:4, :], lv[:, 2:4, :], ACT.Exp).then_inc(s_exp.sem, 1)

            @block.tensor
            def _(pe):
                pe.wait_ge(loaded.sem, loaded.at(80))
                for t in range(NT):
                    pe.wait_ge(norm.ready.sem, norm.ready.at(t + 1))
                    for half in range(2):
                        n = 2 * t + half
                        if n >= 2:
                            pe.wait_ge(s_h.sem, s_h.at(n - 1))
                        for j in range(4):
                            mm = pe.transpose(bank[:, n % 2, j * P:(j + 1) * P], norm.h[:, t % norm.ring, 4 * half + j:D:J], K.ident[:])
                        mm.then_inc(norm.turned.sem, 1)
                    pe.wait_ge(s_h.sem, s_h.at(2 * t + 2))
                    for j in range(J):
                        mm = pe.matmul(lg[:, t, :], h32[:, j, :], rw[:, j, :], start=j == 0, stop=j == J - 1)
                    mm.then_inc(s_log.sem, 1)
                pe.wait_ge(s_v.sem, s_v.at(V_CHOSEN))
                for t in range(NT):
                    for u in range(t):
                        pe.matmul(rk[:, t, :], ones[:], ms[:, u, :], start=u == 0, stop=False)
                    pe.matmul(rk[:, t, :], mask[:], ms[:, t, :], start=t == 0, stop=True)
                for t in range(NT):
                    mm = pe.matmul(ct_[:], ones[:], ms[:, t, :], start=t == 0, stop=t == NT - 1)
                mm.then_inc(s_rank.sem, 1)

            @block.vector
            def _(dve):
                dve.memset(ones[:], 1.0)
                norm.rows(dve)

                def step(ins):
                    steps[0] += 1
                    ins.then_inc(s_v.sem, 1)
                    dve.wait_ge(s_v.sem, s_v.at(steps[0]))

                def tiles(ap, n=NT):
                    return ap.rearrange("p (o e) -> p o e", o=1).broadcast_to([P, n, E])

                def each(ap):
                    return ap.rearrange("p (t o) -> p t o", o=1).broadcast_to([P, NT, E])

                dve.wait_ge(s_log.sem, s_log.at(NT))
                dve.wait_ge(loaded.sem, loaded.at(80))
                step(dve.tensor_copy(logits[:], lg[:]))
                step(dve.tensor_tensor(biased[:], logits[:], tiles(rb[:]), ALU.add))
                for t in range(NT):
                    step(dve.max(mx[:, t, :], biased[:, t, :]))
                    step(dve.max_index(ix[:, t, :], mx[:, t, :], biased[:, t, :]))
                step(dve.tensor_copy(ixf[:], ix[:, :, 0:2]))
                for c, m in enumerate((m1, m2)):
                    step(dve.tensor_tensor(m[:], each(ixf[:, :, c]), tiles(small[:, 0:E]), ALU.is_equal))
                    step(dve.tensor_tensor(tmp[:], m[:], logits[:], ALU.mult))
                    step(dve.tensor_reduce(lv[:, c, :], tmp[:], AX.X, ALU.add))
                step(dve.tensor_tensor(ms[:], m1[:], m2[:], ALU.add))
                assert steps[0] == V_CHOSEN, steps
                step(dve.tensor_tensor(lv[:, 4, :], lv[:, 0, :], lv[:, 1, :], ALU.max))
                for c in range(2):
                    step(dve.tensor_tensor(lv[:, 2 + c, :], lv[:, c, :], lv[:, 4, :], ALU.subtract))
                assert steps[0] == V_EXP, steps
                dve.wait_ge(s_exp.sem, s_exp.at(1))
                step(dve.tensor_tensor(lv[:, 4, :], lv[:, 2, :], lv[:, 3, :], ALU.add))
                step(dve.reciprocal(lv[:, 5, :], lv[:, 4, :]))
                for c in range(2):
                    step(dve.tensor_tensor(K.weight[:, c, :], lv[:, 2 + c, :], lv[:, 5, :], ALU.mult))
                dve.wait_ge(s_rank.sem, s_rank.at(1))
                step(dve.tensor_copy(cnt[:], ct_[:]))
                for m in range(NT):
                    step(dve.tensor_scalar(part[:, m, :], cnt[:], float(m * P), None, ALU.is_gt))
                step(dve.tensor_reduce(nt[:], part[:].rearrange("p m e -> p e m"), AX.X, ALU.add))
                step(dve.tensor_tensor_scan(incl[:], ones[:, 0:E], nt[:], 0.0, ALU.mult, ALU.add))
                step(dve.tensor_tensor(nt[:], incl[:], nt[:], ALU.subtract))
                step(dve.scalar_tensor_tensor(pos[:], tiles(nt[:]), float(P), rk[:], ALU.mult, ALU.add))
                for c, m in enumerate((m1, m2)):
                    step(dve.tensor_tensor(tmp[:], m[:], pos[:], ALU.mult))
                    step(dve.tensor_reduce(lv[:, c, :], tmp[:], AX.X, ALU.add))
                    step(dve.tensor_scalar(K.slot[:, c, :], lv[:, c, :], float(P), None, ALU.add))
                step(dve.tensor_tensor(te[:], tiles(incl[:], SLOT_TILES),
                                       small[:, 8:8 + SLOT_TILES].rearrange("p (t o) -> p t o", o=1).broadcast_to([P, SLOT_TILES, E]), ALU.is_le))
                step(dve.tensor_reduce(tef[:], te[:], AX.X, ALU.add))
                step(dve.tensor_scalar(expert_of[:], tef[:], float(E - 1), None, ALU.min))
                assert steps[0] == V_ALL, steps

            @block.gpsimd
            def _(pool):
                pool.memset(zero[:], 0).then_inc(s_z.sem, 1)
                norm.rstds(pool)
                pool.wait_ge(s_v.sem, s_v.at(V_ALL))
                pool.wait_ge(s_cleared.sem, s_cleared.at(16))
                pool.wait_ge(loaded.sem, loaded.at(80))
                for c in range(2):
                    for t in range(NT):
                        pool.indirect_dma_start(K.tokens_of_slots[:, :], bass.IndirectOffsetOnAxis(ap=K.slot[:, c, t:t + 1], axis=0),
                                                tok[:, t:t + 1], None).then_inc(s_scatter.sem, 16)
                pool.wait_ge(s_scatter.sem, s_scatter.at(16 * 2 * NT))
        norm.end()
        loaded.base += 80
        s_cleared.base += 16
        s_scatter.base += 16 * 2 * NT
        s_v.base += V_ALL
        for s, n in ((s_log, NT), (s_rank, 1), (s_z, 1), (s_exp, 1), (s_h, 2 * NT)):
            s.base += n


V_CHOSEN = 2 + 2 * NT + 1 + 6 + 1
V_EXP = V_CHOSEN + 3
V_ALL = V_EXP + 4 + 1 + NT + 4 + 6 + 3


def experts_stage(K, expert_of):
    nc, I = K.nc, K.I
    CH, KU = D_EXPERT // ECH, J // 2
    GU, DN = CH * KU, D_EXPERT // P
    NU = GU + DN
    NTURN = CH + 2
    TA = ((0, 2), (2, 5), (5, 8), (8, 11))
    assert NU % MRAW == 0 and NU % MSPLIT == 0
    with ExitStack() as ctx:
        raw = K.sb(ctx, "m_raw", [P, MRAW, MUNIT])
        whi, wlo = K.sb(ctx, "m_hi", [P, MSPLIT, MUNIT], F32R), K.sb(ctx, "m_lo", [P, MSPLIT, MUNIT], F32R)
        xg = K.sb(ctx, "x_gathered", [P, D])
        xh, xl = K.sb(ctx, "x_hi", [P, J, P], F32R), K.sb(ctx, "x_lo", [P, J, P], F32R)
        silu = K.sb(ctx, "m_silu", [P, ECH])
        act = K.sb(ctx, "m_act", [P, D_EXPERT])
        ah, al = K.sb(ctx, "m_a_hi", [P, DN, P], F32R), K.sb(ctx, "m_a_lo", [P, DN, P], F32R)
        ysb = K.sb(ctx, "y_slot", [P, D])
        idx = K.sb(ctx, "slot_tokens", [P, SLOT_TILES + 1], I32)
        pG, pU = K.ps(ctx, "p_gates", [P, 2, 512]), K.ps(ctx, "p_ups", [P, 2, 512])
        pT, pD = K.ps(ctx, "p_turned", [P, 2, 512]), K.ps(ctx, "p_down", [P, 2, 512])
        landed = [K.sig(f"m_landed{s}") for s in range(MRAW)]
        names = ("hi", "lo", "used", "silu", "act", "turned", "t_hi", "t_lo", "y")
        s_hi, s_lo, s_used, s_silu, s_act, s_turned, s_thi, s_tlo, s_y = (K.sig("m_" + n) for n in names)
        s_clear = K.sig("rt_zero")
        s_stored, s_idx, s_gather = K.sig("m_stored"), K.sig("m_slots"), K.sig("m_gathered")
        wgu = I["moe_w_gu"][0].rearrange("e (p j) (h n) -> e p j h n", j=J, h=2)
        wdn = I["moe_w_dn"][0].rearrange("e (j p) n -> e p j n", p=P)

        def gu(ring, u):
            return ring[:, u % ring.shape[1], :].rearrange("p (j h n) -> p j h n", j=2, h=2)

        def size(u):
            return MUNIT if u < GU else D

        with nc.Block() as block:
            @block.sync
            def _(sp):
                with sp.Fori(0, SLOT_TILES) as tile:
                    e = sp.value_load(expert_of[0:1, bass.ds(tile, 1)], min_val=0, max_val=N_EXP - 1)
                    for u in range(NU):
                        sp.wait_ge(s_lo.sem, s_lo.at(tile * NU + (u - MRAW + 1)))
                        s = u % MRAW
                        if u < GU:
                            c, k = divmod(u, KU)
                            for b in range(2):
                                src = wgu[bass.ds(e, 1), :, 2 * k + b, :, c * ECH:(c + 1) * ECH].rearrange("e p h n -> p (e h) n")
                                sp.dma_start(gu(raw, u)[:, b], src).then_inc(landed[s].sem, 16)
                        else:
                            src = wdn[bass.ds(e, 1), :, u - GU, :].rearrange("e p n -> p (e n)")
                            sp.dma_start(raw[:, s, 0:D], src).then_inc(landed[s].sem, 32)

            @block.gpsimd
            def _(pool):
                with nc.allow_non_contiguous_dma("one token number to a slot"):
                    pool.dma_start(idx[:], K.tokens_of_slots[P:SLOTS, :].rearrange("(t p) o -> p (t o)", p=P)).then_inc(s_idx.sem, 16)
                pool.wait_ge(s_idx.sem, s_idx.at(16))
                for tile in range(SLOT_TILES + 1):
                    if tile:
                        pool.wait_ge(s_turned.sem, s_turned.at(2 if tile == 1 else NTURN * (tile - 2) + 7))
                    pool.indirect_dma_start(xg[:, :], None, K.h_rows[:, :],
                                            bass.IndirectOffsetOnAxis(ap=idx[:, tile:tile + 1], axis=0)).then_inc(s_gather.sem, 16)
                pool.wait_ge(s_gather.sem, s_gather.at(16 * (SLOT_TILES + 1)))

            def use(tile, j):
                return NTURN * tile + (2 + j)

            X_USES, A_USES = (3, 4), (0, 1, 2, 5)

            @block.tensor
            def _(pe):
                def turn_x(n, half, first=False):
                    if not first:
                        pe.wait_ge(s_tlo.sem, s_tlo.at(n - 1))
                    for j in range(4):
                        mm = pe.transpose(pT[:, half ^ (0 if first else 1), j * P:(j + 1) * P], xg[:, 4 * half + j:D:J], K.ident[:])
                    mm.then_inc(s_turned.sem, 1)

                def turn_a(tile, c):
                    a, b = TA[c]
                    pe.wait_ge(s_act.sem, s_act.at(tile * CH + (c + 1)))
                    pe.wait_ge(s_tlo.sem, s_tlo.at(use(tile, A_USES[c]) - 1))
                    for j in range(a, b):
                        mm = pe.transpose(pT[:, A_USES[c] % 2, (j - a) * P:(j - a + 1) * P], act[:, j * P:(j + 1) * P], K.ident[:])
                    mm.then_inc(s_turned.sem, 1)

                pe.wait_ge(s_gather.sem, s_gather.at(16))
                for half in range(2):
                    turn_x(half, half, first=True)
                with pe.Fori(0, SLOT_TILES) as tile:
                    pe.wait_ge(s_tlo.sem, s_tlo.at(NTURN * tile + 2))
                    for u in range(NU):
                        s = u % MSPLIT
                        if u < GU:
                            c, k = divmod(u, KU)
                            if k == 0:
                                pe.wait_ge(s_act.sem, s_act.at(tile * CH + (c - 1)))
                            pe.wait_ge(s_lo.sem, s_lo.at(tile * NU + (u + 1)))
                            h, l = gu(whi, u), gu(wlo, u)
                            for b in range(2):
                                j = 2 * k + b
                                start, stop = j == 0, j == J - 1
                                for half, bank in ((0, pG), (1, pU)):
                                    pe.matmul(bank[:, c % 2, 0:ECH], xh[:, j, :], h[:, b, half, :], start=start, stop=False)
                                    pe.matmul(bank[:, c % 2, 0:ECH], xh[:, j, :], l[:, b, half, :], start=False, stop=False)
                                for half, bank in ((0, pG), (1, pU)):
                                    mm = pe.matmul(bank[:, c % 2, 0:ECH], xl[:, j, :], h[:, b, half, :], start=False, stop=stop)
                            mm.then_inc(s_used.sem, 1)
                        else:
                            k = u - GU
                            if k == 0:
                                pe.wait_ge(s_y.sem, s_y.at(tile + 1))
                                pe.wait_ge(s_tlo.sem, s_tlo.at(use(tile, 2) + 1))
                            if k == TA[3][0]:
                                pe.wait_ge(s_tlo.sem, s_tlo.at(use(tile, 5) + 1))
                            pe.wait_ge(s_lo.sem, s_lo.at(tile * NU + (u + 1)))
                            for half in range(2):
                                cs = slice(half * 512, half * 512 + 512)
                                pe.matmul(pD[:, half, :], ah[:, k, :], whi[:, s, cs], start=k == 0, stop=False)
                                pe.matmul(pD[:, half, :], ah[:, k, :], wlo[:, s, cs], start=False, stop=False)
                            for half in range(2):
                                cs = slice(half * 512, half * 512 + 512)
                                mm = pe.matmul(pD[:, half, :], al[:, k, :], whi[:, s, cs], start=False, stop=k == DN - 1)
                            mm.then_inc(s_used.sem, 1)
                        if u in (7, 11, 15):
                            turn_a(tile, (u - 7) // 4)
                        if u == 16:
                            pe.wait_ge(s_gather.sem, s_gather.at(tile * 16 + 32))
                            for half in range(2):
                                turn_x(use(tile, X_USES[half]), half)
                        if u == 19:
                            turn_a(tile, 3)

            @block.scalar
            def _(a):
                def part_x(n, half, bank):
                    a.wait_ge(s_turned.sem, s_turned.at(n + 1))
                    a.activation(xh[:, 4 * half:4 * half + 4, :], pT[:, bank, :].rearrange("p (j n) -> p j n", j=4), ACT.Copy).then_inc(s_thi.sem, 1)

                def part_a(tile, c):
                    x, y = TA[c]
                    a.wait_ge(s_turned.sem, s_turned.at(use(tile, A_USES[c]) + 1))
                    a.activation(ah[:, x:y, :], pT[:, A_USES[c] % 2, 0:(y - x) * P].rearrange("p (j n) -> p j n", n=P), ACT.Copy).then_inc(s_thi.sem, 1)

                for half in range(2):
                    part_x(half, half, half)
                a.wait_ge(s_clear.sem, s_clear.at(1))
                with a.Fori(0, SLOT_TILES) as tile:
                    for u in range(NU):
                        s = u % MRAW
                        a.wait_ge(landed[s].sem, landed[s].at((tile * (NU // MRAW) + (u // MRAW + 1)) * 32))
                        a.wait_ge(s_used.sem, s_used.at(tile * NU + (u - MSPLIT + 1)))
                        a.activation(whi[:, u % MSPLIT, 0:size(u)], raw[:, s, 0:size(u)], ACT.Copy).then_inc(s_hi.sem, 1)
                        if u == 2:
                            a.wait_ge(s_used.sem, s_used.at(tile * NU))
                            a.wait_ge(s_stored.sem, s_stored.at(tile * 16))
                            a.activation(ysb[:], pD[:].rearrange("p h n -> p (h n)"), ACT.Copy).then_inc(s_y.sem, 1)
                            a.wait_ge(s_y.sem, s_y.at(tile + 1))
                            a.dma_start(K.y_slots[bass.ds(tile * P, P), :], ysb[:]).then_inc(s_stored.sem, 16)
                        if u in (6, 10, 14, 18):
                            c = u // 4 - 1
                            a.wait_ge(s_used.sem, s_used.at(tile * NU + 4 * (c + 1)))
                            a.wait_ge(s_act.sem, s_act.at(tile * CH + c))
                            a.activation(silu[:], pG[:, c % 2, 0:ECH], ACT.Silu).then_inc(s_silu.sem, 1)
                        if u in (9, 13, 17, 21):
                            part_a(tile, u // 4 - 2)
                        if u == 19:
                            for half in range(2):
                                part_x(use(tile, X_USES[half]), half, half ^ 1)
                n = SLOT_TILES
                a.wait_ge(s_used.sem, s_used.at(n * NU))
                a.wait_ge(s_stored.sem, s_stored.at(16 * n))
                a.activation(ysb[:], pD[:].rearrange("p h n -> p (h n)"), ACT.Copy).then_inc(s_y.sem, 1)
                a.wait_ge(s_y.sem, s_y.at(n + 1))
                a.dma_start(K.y_slots[n * P:(n + 1) * P, :], ysb[:]).then_inc(s_stored.sem, 16)
                a.wait_ge(s_stored.sem, s_stored.at(16 * (n + 1)))

            @block.vector
            def _(dve):
                def part_x(n, half, bank):
                    dve.wait_ge(s_thi.sem, s_thi.at(n + 1))
                    at = slice(4 * half, 4 * half + 4)
                    dve.tensor_tensor(xl[:, at, :], pT[:, bank, :].rearrange("p (j n) -> p j n", j=4), xh[:, at, :], ALU.subtract).then_inc(s_tlo.sem, 1)

                def part_a(tile, c):
                    x, y = TA[c]
                    dve.wait_ge(s_thi.sem, s_thi.at(use(tile, A_USES[c]) + 1))
                    dve.tensor_tensor(al[:, x:y, :], pT[:, A_USES[c] % 2, 0:(y - x) * P].rearrange("p (j n) -> p j n", n=P),
                                      ah[:, x:y, :], ALU.subtract).then_inc(s_tlo.sem, 1)

                dve.memset(pD[:], 0.0).then_inc(s_clear.sem, 1)
                for half in range(2):
                    part_x(half, half, half)
                with dve.Fori(0, SLOT_TILES) as tile:
                    for u in range(NU):
                        dve.wait_ge(s_hi.sem, s_hi.at(tile * NU + (u + 1)))
                        n = size(u)
                        dve.tensor_tensor(wlo[:, u % MSPLIT, 0:n], raw[:, u % MRAW, 0:n], whi[:, u % MSPLIT, 0:n], ALU.subtract).then_inc(s_lo.sem, 1)
                        if u in (6, 10, 14, 18):
                            c = u // 4 - 1
                            dve.wait_ge(s_silu.sem, s_silu.at(tile * CH + (c + 1)))
                            dve.tensor_tensor(act[:, c * ECH:(c + 1) * ECH], silu[:], pU[:, c % 2, 0:ECH], ALU.mult).then_inc(s_act.sem, 1)
                        if u in (9, 13, 17, 21):
                            part_a(tile, u // 4 - 2)
                        if u == 19:
                            for half in range(2):
                                part_x(use(tile, X_USES[half]), half, half ^ 1)
        n = SLOT_TILES
        for s in landed:
            s.base += 32 * n * (NU // MRAW)
        for s, k in ((s_hi, NU), (s_lo, NU), (s_used, NU), (s_silu, CH), (s_act, CH), (s_y, 1), (s_stored, 16)):
            s.base += k * n
        s_y.base += 1
        s_stored.base += 16
        s_clear.base += 1
        s_idx.base += 16
        s_gather.base += 16 * (n + 1)
        for s in (s_turned, s_thi, s_tlo):
            s.base += NTURN * n + 2


def combine_stage(K):
    nc, I, O = K.nc, K.I, K.O
    with ExitStack() as ctx:
        gate = K.sb(ctx, "gate", [P, 2, D])
        g = K.sb(ctx, "final_g", [P, D])
        picked = K.sb(ctx, "picked_rows", [P, NT, 2, D])
        junk = K.sb(ctx, "squares", [P, D])
        out = K.sb(ctx, "out_rows", [P, NT, D])
        ss = K.sb(ctx, "final_ss", [P, 3, NT])
        loaded, s_v = K.sig("loaded"), K.sig("gn_steps")
        gathered = [K.sig(n) for n in ("cb_gathered0", "cb_gathered1", "rt_scattered", "m_gathered", "m_slots")]
        s_sq, s_mean, s_rstd, s_out, s_store = K.sig("norm_square"), K.sig("norm_mean"), K.sig("norm_rstd"), K.sig("norm_h"), K.sig("ada_stored0")
        s_weighted = K.sig("rt_exp")
        with nc.Block() as block:
            @block.sync
            def _(sp):
                for cond in range(2):
                    at = (1 * 6 + 5) * D
                    sp.dma_start(gate[:, cond, :], K.mods[cond:cond + 1, at:at + D].broadcast_to([P, D])).then_inc(loaded.sem, 16)
                sp.dma_start(g[:], I["final_norm_g"].rearrange("(o n) -> o n", o=1).broadcast_to([P, D])).then_inc(loaded.sem, 16)
                for t in range(NT):
                    sp.wait_ge(s_out.sem, s_out.at(t + 1))
                    dst = O["y_prompt"][0] if t == 0 else O["y_sample"][0, (t - 1) * P:t * P, :]
                    sp.dma_start(dst, out[:, t, :]).then_inc(s_store.sem, 16)
                sp.wait_ge(s_store.sem, s_store.at(16 * NT))

            @block.gpsimd
            def _(pool):
                for t in range(NT):
                    for c in range(2):
                        pool.indirect_dma_start(picked[:, t, c, :], None, K.y_slots[:, :],
                                                bass.IndirectOffsetOnAxis(ap=K.slot[:, c, t:t + 1], axis=0)).then_inc(gathered[t].sem, 16)
                for t in range(NT):
                    pool.wait_ge(s_sq.sem, s_sq.at(t + 1))
                    pool.tensor_scalar(ss[:, 1, t:t + 1], ss[:, 0, t:t + 1], 1.0 / D, EPS, ALU.mult, ALU.add).then_inc(s_mean.sem, 1)
                    pool.wait_ge(s_mean.sem, s_mean.at(t + 1))
                    pool.tensor_tensor(ss[:, 2, t:t + 1], ss[:, 1, t:t + 1], K.minus_half[:], ALU.pow).then_inc(s_rstd.sem, 1)

            @block.scalar
            def _(a):
                def weigh(t):
                    a.wait_ge(gathered[t].sem, gathered[t].at(32))
                    a.activation(picked[:, t, 0, :], picked[:, t, 0, :], ACT.Copy, scale=K.weight[:, 0, t:t + 1]).then_inc(s_weighted.sem, 1)

                weigh(0)
                for t in range(NT):
                    if t + 1 < NT:
                        weigh(t + 1)
                    a.wait_ge(s_v.sem, s_v.at(3 * (t + 1)))
                    if t:
                        a.wait_ge(s_sq.sem, s_sq.at(t))
                    a.activation(junk[:], K.x[:, t, :], ACT.Square, accum_out=ss[:, 0, t:t + 1]).then_inc(s_sq.sem, 1)

            @block.vector
            def _(dve):
                def step(ins, n):
                    ins.then_inc(s_v.sem, 1)
                    dve.wait_ge(s_v.sem, s_v.at(n))

                def finish(t):
                    dve.wait_ge(s_rstd.sem, s_rstd.at(t + 1))
                    dve.scalar_tensor_tensor(out[:, t, :], K.x[:, t, :], ss[:, 2, t:t + 1], g[:], ALU.mult, ALU.mult).then_inc(s_out.sem, 1)

                dve.wait_ge(loaded.sem, loaded.at(48))
                for t in range(NT):
                    dve.wait_ge(gathered[t].sem, gathered[t].at(32))
                    dve.wait_ge(s_weighted.sem, s_weighted.at(t + 1))
                    y0, y1, x = picked[:, t, 0, :], picked[:, t, 1, :], K.x[:, t, :]
                    step(dve.scalar_tensor_tensor(y0, y1, K.weight[:, 1, t:t + 1], y0, ALU.mult, ALU.add), 3 * t + 1)
                    step(dve.tensor_tensor(y0, y0, gate[:, 1 if t else 0, :], ALU.mult), 3 * t + 2)
                    step(dve.tensor_tensor(x, x, y0, ALU.add), 3 * t + 3)
                    if t:
                        finish(t - 1)
                finish(NT - 1)



def build_program(nc, I, O):
    with ExitStack() as ctx:
        K = Kit(nc, ctx, I, O)
        K.mods = K.dram("mods", [2, 12 * D])
        K.h_rows = K.dram("h_rows", [T, D])
        K.x_rows = K.dram("x_rows", [P, NT, D])
        K.rpb_rows = K.dram("rpb_rows", [C_HEADS * 15, P])
        K.tokens_of_slots = K.dram("tokens_of_slots", [SLOTS, 1], I32)
        K.y_slots = K.dram("y_slots", [(SLOT_TILES + 1) * P, D])
        K.x = K.sb(ctx, "x", [P, NT, D])
        K.ident = K.sb(ctx, "ident", [P, P])
        K.ones = K.sb(ctx, "ones", [P, 1])
        K.minus_half = K.sb(ctx, "minus_half", [P, 1])
        K.slot = K.sb(ctx, "slot_of_choice", [P, 2, NT], I32)
        K.weight = K.sb(ctx, "weight_of_choice", [P, 2, NT])
        expert_of = K.sb(ctx, "expert_of_tile", [P, SLOT_TILES], I32)
        prime(K)
        adaln_stage(K)

        def part(h):
            return lambda j, t: h[:, j, t * P:(t + 1) * P]

        def close_mixer(layer, w, turn=None):
            output_stage(K, layer, 2, w, rows_by_block, J // 2, turn, hi=part(K.h_hi), lo=part(K.h_lo))

        with ExitStack() as even:
            K.transposed_rows(even)
            with ExitStack() as mixed:
                zs = K.sb(mixed, "zs", [P, ZT, T])
                with ExitStack() as rows:
                    z = K.sb(rows, "z", [P, NT, EVEN_IN])
                    project_stage(K, 0, I["w_in_e"][0], 7, EVEN_IN // 7, z, together=False)
                    shift_stage(K, z, zs)
                    even_attention_stage(K, z)
                rwkv_stage(K, zs)
            close_mixer(0, I["w_out_e"][0])
        ffn_stage(K)
        with ExitStack() as odd:
            K.transposed_rows(odd)
            with ExitStack() as rows:
                z = K.sb(rows, "z", [P, NT, 3 * D])
                project_stage(K, 1, I["w_in_o"][0], 6, 512, z, together=True)
                flip = K.sb(rows, "flip", [P, P])
                odd_attention_stage(K, z, flip)
                turn = Turn(K, lambda t, b: z[:, t, b * P:(b + 1) * P], J, 0, K.ps(rows, "turn_bank", [P, 2, 512]), flip)
                close_mixer(1, I["w_out_o"][0], turn)
            route_stage(K, expert_of)
        experts_stage(K, expert_of)
        combine_stage(K)


def shape_constants():
    f = np.float32
    p = np.arange(P)
    c = {"const_ident": np.eye(P, dtype=f)}
    c["const_head_ones"] = (p[:, None] // HD == p[None, :] // HD).astype(f)
    c["const_flip"] = (p[:, None] == p[None, :] // HD * HD + HD - 1 - p[None, :] % HD).astype(f)
    before, upto = p[:, None] < p[None, :], p[:, None] <= p[None, :]
    m = [np.concatenate([a, b], axis=1) for a, b in ((before, upto), (before.T, upto.T))]
    c["const_masks"] = np.stack(m, axis=1).astype(f)
    t = np.arange(T - P)
    inv = 10000.0 ** (-np.arange(16, dtype=f) / 16)
    ang = [pos[:, None].astype(f) * inv[None, :] for pos in (t // 64, t % 64)]
    cos = np.concatenate([np.cos(a) for a in ang for _ in range(2)], axis=1)
    sin = np.concatenate([s * np.sin(a) for a in ang for s in (-1, 1)], axis=1)
    rope = np.stack([cos, sin], axis=1).astype(f).reshape(NT - 1, P, 2, HD)
    c["const_rope"] = np.ascontiguousarray(rope.transpose(1, 0, 2, 3))
    q, k = HD - 1 - p % HD, np.arange(HD)
    cs = np.clip(q - 8, 0, HD - 16)
    inside = (k[None, :] >= cs[:, None]) & (k[None, :] < cs[:, None] + 16)
    c["const_outside"] = np.where(inside, 0.0, -1e30).astype(f)
    iotas = np.zeros((P, 40), f)
    iotas[:, 0:8] = np.arange(8)
    iotas[:, 8:8 + SLOT_TILES] = np.arange(SLOT_TILES)
    c["const_iotas"] = iotas
    c["const_tokens"] = (np.arange(NT)[None, :] * P + p[:, None]).astype(np.int32)
    return c


_INS = ["x_prompt", "x_sample", "cache_a_k", "cache_a_v", "state_b_fwd", "state_b_bwd", "cache_c_k", "cache_c_v",
        "c", "c_ctx", "ada_w", "ada_b", "norm1_g", "norm2_g", "final_norm_g", "w_in_e", "w_out_e", "a_q_gain", "a_k_gain",
        "b_mu", "b_w0", "b_w2", "b_a0", "b_a2", "b_g2", "b_kk", "b_ka", "b_rk", "b_ln_g", "b_ln_b", "ffn_w_gu", "ffn_w_dn",
        "w_in_o", "w_out_o", "c_rpb", "router_w", "router_b", "moe_w_gu", "moe_w_dn"]
_OUTS = [("y_prompt", (1, P, D)), ("y_sample", (1, T - P, D)),
         ("new_cache_a_k", (1, 1, P, A_KV, HD)), ("new_cache_a_v", (1, 1, P, A_KV, HD)),
         ("new_state_b_fwd", (1, 1, B_HEADS, HD, HD)), ("new_state_b_bwd", (1, 1, B_HEADS, HD, HD)),
         ("new_cache_c_k", (1, 1, P, C_HEADS, HD)), ("new_cache_c_v", (1, 1, P, C_HEADS, HD))]


def kernel(**inputs):
    import concourse.bacc as bacc
    from concourse.bass_utils import run_bass_kernel_spmd

    nc = bacc.Bacc("TRN2", target_bir_lowering=False, num_devices=1)
    arrays = {name: np.ascontiguousarray(inputs[name]) for name in _INS} | shape_constants()
    ins = {name: nc.dram_tensor(name, a.shape, mybir.dt.from_np(a.dtype), kind="ExternalInput").ap() for name, a in arrays.items()}
    outs = {name: nc.dram_tensor("out_" + name, shape, F32, kind="ExternalOutput").ap() for name, shape in _OUTS}
    build_program(nc, ins, outs)
    r = run_bass_kernel_spmd(nc, [arrays], core_ids=[0])
    return tuple(r.results[0]["out_" + name] for name, _ in _OUTS)
```
